# Optimizing a Trainium2 kernel written in Bass

```python
import math
import jax, jax.numpy as jnp
from jax import lax
import numpy as np

D_MODEL = 2048
BATCH = 1
SEQ = 256
DEPTH = 1

HEAD_DIM = 64
A_HEADS = 16
A_KV_HEADS = 4
A_WINDOW = 128
A_BLOCK = 128
B_HEADS = 8
B_BLOCK = 256
B_TOPK = 3
B_QCHUNK = 32
C_HEADS = 8
C_LATENT = 128
IDX_HEADS = 8
IDX_DIM = 32
C_TOPK_MAX = 256
C_QCHUNK = 128
REL_BUCKETS = 32
REL_MAX_DIST = 2048
N_ATTN_HEADS = A_HEADS + B_HEADS + C_HEADS
PEER_HEADS = 8
PEER_KEYS = 128
PEER_N = PEER_KEYS * PEER_KEYS
PEER_QDIM = 256
PEER_TOPK = 16
PEER_TCHUNK = 128
EPS = 1e-6
NEG = -1e30

IN_SPLITS = (A_HEADS * HEAD_DIM, A_KV_HEADS * HEAD_DIM, A_KV_HEADS * HEAD_DIM,
             B_HEADS * HEAD_DIM, B_HEADS * HEAD_DIM, B_HEADS * HEAD_DIM,
             C_HEADS * HEAD_DIM, C_LATENT, IDX_HEADS * IDX_DIM, IDX_DIM, IDX_HEADS,
             D_MODEL, D_MODEL, D_MODEL)
IN_COLS = sum(IN_SPLITS)

kernel_name = "hybrid_gated_swa_moba_dsa_peer"

def rmsnorm(x, g):
    x32 = x.astype(jnp.float32)
    y = x32 * lax.rsqrt(jnp.mean(x32 * x32, axis=-1, keepdims=True) + EPS)
    return (y * g.astype(jnp.float32)).astype(x.dtype)

def rel_bucket(dist):
    d = jnp.maximum(dist, 0)
    max_exact = REL_BUCKETS // 2
    df = jnp.maximum(d, max_exact).astype(jnp.float32)
    large = max_exact + (jnp.log(df / max_exact) / math.log(REL_MAX_DIST / max_exact)
                         * (REL_BUCKETS - max_exact)).astype(jnp.int32)
    large = jnp.minimum(large, REL_BUCKETS - 1)
    return jnp.where(d < max_exact, d, large)

def swa_sink_attention(q, k, v, sinks, bt):
    B, T = q.shape[0], q.shape[1]
    nq = T // A_BLOCK
    G = A_HEADS // A_KV_HEADS
    qb = q.reshape(B, nq, A_BLOCK, A_KV_HEADS, G, HEAD_DIM)
    pad = jnp.zeros((B, A_BLOCK, A_KV_HEADS, HEAD_DIM), k.dtype)
    kp = jnp.concatenate([pad, k], axis=1).reshape(B, nq + 1, A_BLOCK, A_KV_HEADS, HEAD_DIM)
    vp = jnp.concatenate([pad.astype(v.dtype), v], axis=1).reshape(B, nq + 1, A_BLOCK, A_KV_HEADS, HEAD_DIM)
    kb = jnp.concatenate([kp[:, :-1], kp[:, 1:]], axis=2)
    vb = jnp.concatenate([vp[:, :-1], vp[:, 1:]], axis=2)
    s = jnp.einsum("bnqhgd,bnkhd->bnhgqk", qb, kb).astype(jnp.float32) * (HEAD_DIM ** -0.5)
    qpos = jnp.arange(A_BLOCK)[:, None] + A_BLOCK
    kpos = jnp.arange(2 * A_BLOCK)[None, :]
    dist = qpos - kpos
    band = (dist >= 0) & (dist < A_WINDOW)
    real = (jnp.arange(nq)[:, None, None] > 0) | (kpos[None] >= A_BLOCK)
    mask = band[None] & real
    bias = bt[rel_bucket(dist)].astype(jnp.float32)
    bias = jnp.transpose(bias, (2, 0, 1)).reshape(A_KV_HEADS, G, A_BLOCK, 2 * A_BLOCK)
    s = jnp.where(mask[None, :, None, None], s + bias[None, None], NEG)
    sink = jnp.broadcast_to(sinks.astype(jnp.float32).reshape(A_KV_HEADS, G, 1, 1)[None, None],
                            s.shape[:-1] + (1,))
    p = jax.nn.softmax(jnp.concatenate([s, sink], axis=-1), axis=-1)[..., :-1]
    o = jnp.einsum("bnhgqk,bnkhd->bnqhgd", p.astype(v.dtype), vb)
    return o.reshape(B, T, A_HEADS * HEAD_DIM)

def moba_attention(q, k, v, bt):
    B, T = q.shape[0], q.shape[1]
    H = B_HEADS
    nb = -(-T // B_BLOCK)
    pad = nb * B_BLOCK - T
    kb = jnp.pad(k, ((0, 0), (0, pad), (0, 0), (0, 0))).reshape(B, nb, B_BLOCK, H, HEAD_DIM).transpose(0, 3, 1, 2, 4)
    vb = jnp.pad(v, ((0, 0), (0, pad), (0, 0), (0, 0))).reshape(B, nb, B_BLOCK, H, HEAD_DIM).transpose(0, 3, 1, 2, 4)
    kmean = jnp.mean(kb.astype(jnp.float32), axis=3)
    qblk = jnp.arange(T) // B_BLOCK
    gate = jnp.einsum("bthd,bhnd->bhtn", q.astype(jnp.float32), kmean)
    past = jnp.arange(nb)[None, :] < qblk[:, None]
    gate = jnp.where(past, gate, NEG)
    topb = min(B_TOPK, nb)
    _, sel = lax.top_k(gate, topb)
    valid = sel < qblk[None, None, :, None]
    nc = T // B_QCHUNK
    qc = q.reshape(B, nc, B_QCHUNK, H, HEAD_DIM).transpose(1, 0, 3, 2, 4)
    selc = sel.reshape(B, H, nc, B_QCHUNK, topb).transpose(2, 0, 1, 3, 4)
    validc = valid.reshape(B, H, nc, B_QCHUNK, topb).transpose(2, 0, 1, 3, 4)
    btT = bt.T.astype(jnp.float32)
    bi = jnp.arange(B)[:, None, None, None]
    hi = jnp.arange(H)[None, :, None, None]
    scale = HEAD_DIM ** -0.5

    def chunk(args):
        c, qx, sx, vx = args
        tq = c * B_QCHUNK + jnp.arange(B_QCHUNK)
        ks = kb[bi, hi, sx]
        vs = vb[bi, hi, sx]
        s_sel = jnp.einsum("bhqd,bhqnkd->bhqnk", qx, ks).astype(jnp.float32) * scale
        pos_sel = sx[..., None] * B_BLOCK + jnp.arange(B_BLOCK)
        b_sel = btT[hi[..., None], rel_bucket(tq[:, None, None] - pos_sel)]
        s_sel = jnp.where(vx[..., None], s_sel + b_sel, NEG).reshape(B, H, B_QCHUNK, topb * B_BLOCK)
        j = (c * B_QCHUNK) // B_BLOCK
        k_own = lax.dynamic_index_in_dim(kb, j, axis=2, keepdims=False)
        v_own = lax.dynamic_index_in_dim(vb, j, axis=2, keepdims=False)
        pos_own = j * B_BLOCK + jnp.arange(B_BLOCK)
        d_own = tq[:, None] - pos_own[None, :]
        s_own = jnp.einsum("bhqd,bhkd->bhqk", qx, k_own).astype(jnp.float32) * scale + btT[:, rel_bucket(d_own)][None]
        s_own = jnp.where((d_own >= 0)[None, None], s_own, NEG)
        p = jax.nn.softmax(jnp.concatenate([s_sel, s_own], axis=-1), axis=-1).astype(v.dtype)
        p_sel = p[..., :topb * B_BLOCK].reshape(B, H, B_QCHUNK, topb, B_BLOCK)
        p_own = p[..., topb * B_BLOCK:]
        return (jnp.einsum("bhqnk,bhqnkd->bhqd", p_sel, vs)
                + jnp.einsum("bhqk,bhkd->bhqd", p_own, v_own))

    o = lax.map(chunk, (jnp.arange(nc), qc, selc, validc))
    return o.transpose(1, 0, 3, 2, 4).reshape(B, T, H * HEAD_DIM)

def dsa_attention(q, c_lat, w_uk, w_uv, iq, ik, iw, bt):
    B, T = q.shape[0], q.shape[1]
    H = C_HEADS
    kc = min(C_TOPK_MAX, T // 4)
    nc = T // C_QCHUNK
    q_abs = jnp.einsum("bthd,chd->bthc", q, w_uk)
    qac = q_abs.reshape(B, nc, C_QCHUNK, H, C_LATENT).transpose(1, 0, 2, 3, 4)
    iqc = iq.reshape(B, nc, C_QCHUNK, IDX_HEADS, IDX_DIM).transpose(1, 0, 2, 3, 4)
    iwc = iw.reshape(B, nc, C_QCHUNK, IDX_HEADS).transpose(1, 0, 2, 3)
    btT = bt.T.astype(jnp.float32)
    kpos = jnp.arange(T)
    bi = jnp.arange(B)[:, None, None]
    hi = jnp.arange(H)[None, :, None, None]
    idx_scale = (IDX_DIM ** -0.5) * (IDX_HEADS ** -0.5)
    scale = HEAD_DIM ** -0.5

    def chunk(args):
        c, qx, iqx, iwx = args
        tq = c * C_QCHUNK + jnp.arange(C_QCHUNK)
        logits = jnp.einsum("bqhd,bsd->bqhs", iqx, ik).astype(jnp.float32)
        score = jnp.einsum("bqh,bqhs->bqs", iwx.astype(jnp.float32), jax.nn.relu(logits)) * idx_scale
        score = jnp.where(kpos[None, None, :] <= tq[None, :, None], score, NEG)
        _, sel = lax.top_k(score, kc)
        c_sel = c_lat[bi, sel]
        dist = tq[None, :, None] - sel
        s = (jnp.einsum("bqhc,bqkc->bhqk", qx, c_sel).astype(jnp.float32) * scale
             + btT[hi, rel_bucket(dist)[:, None]])
        s = jnp.where((dist >= 0)[:, None], s, NEG)
        p = jax.nn.softmax(s, axis=-1).astype(c_lat.dtype)
        oc = jnp.einsum("bhqk,bqkc->bqhc", p, c_sel)
        return jnp.einsum("bqhc,chd->bqhd", oc, w_uv).reshape(B, C_QCHUNK, H * HEAD_DIM)

    o = lax.map(chunk, (jnp.arange(nc), qac, iqc, iwc))
    return o.transpose(1, 0, 2, 3).reshape(B, T, H * HEAD_DIM)

def peer_ffn(h, w_q, sub_keys, u_tab, v_tab):
    B, T, D = h.shape
    n = B * T
    xt = h.reshape(n, D)
    q = (xt @ w_q).reshape(n, PEER_HEADS, 2, PEER_QDIM // 2)
    s = jnp.einsum("nhpd,hpkd->nhpk", q, sub_keys).astype(jnp.float32)
    s1, i1 = lax.top_k(s[:, :, 0], PEER_TOPK)
    s2, i2 = lax.top_k(s[:, :, 1], PEER_TOPK)
    cand_s = (s1[..., :, None] + s2[..., None, :]).reshape(n, PEER_HEADS, PEER_TOPK * PEER_TOPK)
    cand_i = (i1[..., :, None] * PEER_KEYS + i2[..., None, :]).reshape(n, PEER_HEADS, PEER_TOPK * PEER_TOPK)
    top_s, pos = lax.top_k(cand_s, PEER_TOPK)
    experts = jnp.take_along_axis(cand_i, pos, axis=-1)
    g = jax.nn.softmax(top_s, axis=-1).astype(h.dtype)
    nch = n // PEER_TCHUNK

    def chunk(args):
        xc, ec, gc = args
        a = jax.nn.gelu(jnp.einsum("td,thkd->thk", xc, u_tab[ec]))
        return jnp.einsum("thk,thkd->td", gc * a, v_tab[ec])

    out = lax.map(chunk, (xt.reshape(nch, PEER_TCHUNK, D),
                          experts.reshape(nch, PEER_TCHUNK, PEER_HEADS, PEER_TOPK),
                          g.reshape(nch, PEER_TCHUNK, PEER_HEADS, PEER_TOPK)))
    return out.reshape(B, T, D)

def setup_inputs(seed: int = 0) -> dict:
    key = jax.random.key(seed)
    ks = jax.random.split(key, 18)

    def nrm(k, shape, scale):
        return jax.random.normal(k, shape, jnp.float32) * scale

    L = DEPTH
    return {
        "x": nrm(ks[0], (BATCH, SEQ, D_MODEL), 1.0),
        "rel_bias": nrm(ks[1], (REL_BUCKETS, N_ATTN_HEADS), 0.5),
        "g_mix": 1.0 + nrm(ks[2], (L, D_MODEL), 0.02),
        "w_in": nrm(ks[3], (L, D_MODEL, IN_COLS), D_MODEL ** -0.5),
        "a_sinks": nrm(ks[4], (L, A_HEADS), 0.5),
        "c_lat_gain": 1.0 + nrm(ks[5], (L, C_LATENT), 0.02),
        "c_w_uk": nrm(ks[6], (L, C_LATENT, C_HEADS, HEAD_DIM), C_LATENT ** -0.5),
        "c_w_uv": nrm(ks[7], (L, C_LATENT, C_HEADS, HEAD_DIM), C_LATENT ** -0.5),
        "w_br_a": nrm(ks[8], (L, A_HEADS * HEAD_DIM, D_MODEL), (A_HEADS * HEAD_DIM) ** -0.5),
        "w_br_b": nrm(ks[9], (L, B_HEADS * HEAD_DIM, D_MODEL), (B_HEADS * HEAD_DIM) ** -0.5),
        "w_br_c": nrm(ks[10], (L, C_HEADS * HEAD_DIM, D_MODEL), (C_HEADS * HEAD_DIM) ** -0.5),
        "w_out": nrm(ks[11], (L, D_MODEL, D_MODEL), D_MODEL ** -0.5),
        "g_ffn": 1.0 + nrm(ks[12], (L, D_MODEL), 0.02),
        "peer_w_q": nrm(ks[13], (L, D_MODEL, PEER_HEADS * PEER_QDIM), D_MODEL ** -0.5),
        "peer_sub_keys": nrm(ks[14], (L, PEER_HEADS, 2, PEER_KEYS, PEER_QDIM // 2), (PEER_QDIM // 2) ** -0.5),
        "peer_u": nrm(ks[15], (L, PEER_N, D_MODEL), D_MODEL ** -0.5),
        "peer_v": nrm(ks[16], (L, PEER_N, D_MODEL), 0.25),
        "g_final": 1.0 + nrm(ks[17], (D_MODEL,), 0.02),
    }

def reference(x, rel_bias, g_mix, w_in, a_sinks, c_lat_gain, c_w_uk, c_w_uv, w_br_a, w_br_b, w_br_c,
              w_out, g_ffn, peer_w_q, peer_sub_keys, peer_u, peer_v, g_final):
    B, T, D = x.shape
    splits = [int(o) for o in np.cumsum(IN_SPLITS)[:-1]]
    bt_a = rel_bias[:, :A_HEADS]
    bt_b = rel_bias[:, A_HEADS:A_HEADS + B_HEADS]
    bt_c = rel_bias[:, A_HEADS + B_HEADS:]
    for l in range(DEPTH):
        h = rmsnorm(x, g_mix[l])
        (qa, ka, va, qb, kb, vb, qc, clat, iq, ik, iw, ga, gb, gc) = jnp.split(h @ w_in[l], splits, axis=-1)
        ya = swa_sink_attention(qa.reshape(B, T, A_HEADS, HEAD_DIM),
                                ka.reshape(B, T, A_KV_HEADS, HEAD_DIM),
                                va.reshape(B, T, A_KV_HEADS, HEAD_DIM), a_sinks[l], bt_a)
        yb = moba_attention(qb.reshape(B, T, B_HEADS, HEAD_DIM),
                            kb.reshape(B, T, B_HEADS, HEAD_DIM),
                            vb.reshape(B, T, B_HEADS, HEAD_DIM), bt_b)
        yc = dsa_attention(qc.reshape(B, T, C_HEADS, HEAD_DIM), rmsnorm(clat, c_lat_gain[l]),
                           c_w_uk[l], c_w_uv[l], iq.reshape(B, T, IDX_HEADS, IDX_DIM), ik, iw, bt_c)
        merged = (jax.nn.sigmoid(ga) * (ya @ w_br_a[l])
                  + jax.nn.sigmoid(gb) * (yb @ w_br_b[l])
                  + jax.nn.sigmoid(gc) * (yc @ w_br_c[l]))
        x = x + merged @ w_out[l]
        x = x + peer_ffn(rmsnorm(x, g_ffn[l]), peer_w_q[l], peer_sub_keys[l], peer_u[l], peer_v[l])
    return rmsnorm(x, g_final)


_drawn_inputs = setup_inputs


def setup_inputs(seed=0):
    import zlib

    import numpy as np

    out = dict(_drawn_inputs(seed))
    spreads = {}
    factors = {'a_sinks': 23.462, 'c_lat_gain': 5.347, 'g_ffn': 10.319, 'g_final': 7.969}
    for name, (base, spread) in spreads.items():
        noise = np.random.default_rng([zlib.crc32(name.encode()), seed]).standard_normal(out[name].shape)
        drawn = base * np.exp(spread * noise) if base else spread * noise
        out[name] = __import__('jax').numpy.asarray(drawn.astype(out[name].dtype))
    for name, factor in factors.items():
        out[name] = (out[name] * factor).astype(out[name].dtype)
    return out
```

```python
import math
from contextlib import ExitStack

import numpy as np

import concourse.bass as bass
from concourse import mybir

F32 = mybir.dt.float32
FR = mybir.dt.float32r
U32 = mybir.dt.uint32
ALU = mybir.AluOpType
ACT = mybir.ActivationFunctionType
AX = mybir.AxisListType

P = 128
T, D = 256, 2048
NT = T // P
NK = D // P
HD = 64
A_HEADS, A_KV, B_HEADS, C_HEADS = 16, 4, 8, 8
A_WINDOW = 128
LATENT, IDX_HEADS, IDX_DIM = 128, 8, 32
C_TOPK = min(256, T // 4)
BUCKETS, MAX_DIST = 32, 2048
PH, PKEYS, PTOP = 8, 128, 16
EPS = 1e-6
NEG = -1e30
SCALE = HD ** -0.5
IDX_SCALE = (IDX_DIM ** -0.5) * (IDX_HEADS ** -0.5)
TAKEN = -3.0e38

QA = 0
KA = QA + A_HEADS * HD
VA = KA + A_KV * HD
QB = VA + A_KV * HD
KB = QB + B_HEADS * HD
VB = KB + B_HEADS * HD
QC = VB + B_HEADS * HD
CL = QC + C_HEADS * HD
IQ = CL + LATENT
IK = IQ + IDX_HEADS * IDX_DIM
GA = IK + IDX_DIM + IDX_HEADS
GB = GA + D
GC = GB + D

NRAW, NHL = 4, 2
FIRST_COLS = [CL, IK, IQ, IQ + P, KA, KA + P, VA, VA + P] + [KB + P * j for j in range(4)] + [VB + P * j for j in range(4)]
N_FIRST = len(FIRST_COLS)
PAIRS = 16
TURNED = [0, 6, 7, 12, 13, 14, 15]
WIDE = 512
NWIDE = D // WIDE
N_BR = N_FIRST + 4 * PAIRS
N_OUT = N_BR + NK
N_WQ = N_OUT + NK
LOOPS = {"a": (0, 4, QA), "b": (4, 2, QB), "c": (6, 2, QC)}
KT_B, KT_C = 4, 8
V_B, V_C = A_KV * HD, A_KV * HD + B_HEADS * HD
V_COLS = V_C + C_HEADS * HD
LAG = 2
W_INC = 48
RING = 4
NU = NT * PH


def bucket_onehots():
    d = 255 - np.arange(384)
    exact = BUCKETS // 2
    far = np.maximum(d, exact).astype(np.float32)
    large = exact + (np.log(far / np.float32(exact)) / np.float32(math.log(MAX_DIST / exact)) * np.float32(BUCKETS - exact)).astype(np.int32)
    bucket = np.where(d < exact, np.maximum(d, 0), np.minimum(large, BUCKETS - 1))
    out = np.zeros((BUCKETS + 1, 2, 384), np.float32)
    for n, keep in enumerate([(d >= 0) & (d < A_WINDOW), d >= 0]):
        out[np.where(keep, bucket, BUCKETS), n, np.arange(384)] = 1.0
    return out


def build(nc, x, rel_bias, g_mix, w_in, a_sinks, c_lat_gain, c_w_uk, c_w_uv, w_br_a, w_br_b, w_br_c,
          w_out, g_ffn, peer_w_q, peer_sub_keys, peer_u, peer_v, g_final, out):
    ctx = ExitStack()
    K = 1024
    base = 16896

    def at(name, kib, shape, dt=F32):
        return nc.alloc_sbuf_tensor_at(name, shape, dt, offset=base + int(kib * K))

    def sem(name):
        return ctx.enter_context(nc.semaphore(name))

    act_hi = at("act_hi", 0, [P, NK, T], FR)
    act_lo = at("act_lo", 16, [P, NK, T], FR)
    w_hi = at("w_hi", 32, [P, NHL, NK, P], FR)
    w_lo = at("w_lo", 48, [P, NHL, NK, P], FR)
    raw = at("raw", 64, [P, NRAW, NK, P])
    raw_wide = raw[:, :, :, :].rearrange("p s (a b) c -> p s a (b c)", b=WIDE // P)
    gates = at("gates", 96, [P, PAIRS * 3 * T])
    yT = at("yT", 144, [P, NK * T])
    kT = at("kT", 160, [P, 12 * T])
    vals = at("vals", 172, [P, NT, V_COLS])
    q_st = at("q_st", 182, [P, 2, 2, T])
    bias_st = at("bias_st", 186, [P, 2, 2, T])
    cbias = at("cbias", 190, [P, 2, 3 * P])
    dsa_mask = at("dsa_mask", 193, [P, 3 * P])
    probs = at("probs", 194.5, [P, 2, 2, 3 * P])
    pT = at("pT", 200.5, [P, 2, 3 * P])
    o_st = at("o_st", 203.5, [P, NT, P])
    ident = at("ident", 204.5, [P, P])
    sinkb = at("sinkb", 205, [P, A_HEADS])
    stat = at("stat", 205.0625, [P, 7, 8])
    smax = at("smax", 205.3125, [P, 2, 2, NT, 2])
    rsum = at("rsum", 205.375, [P, 2, NT, 2])
    esink = at("esink", 205.40625, [P, 2, NT, 2])
    xin = at("xin", 96, [P, NT, D])
    junk0 = at("junk0", 112, [P, D])
    ikz = at("ikz", 120, [P, 4, T])
    iqT = at("iqT", 124, [P, 2, T])
    ikwT = at("ikwT", 126, [P, T])
    iw = at("iw", 127, [P, NT, IDX_HEADS])
    clat = at("clat", 127.25, [P, NT, P])
    cT = at("cT", 128.25, [P, T])
    w_uk = at("w_uk", 129.25, [P, C_HEADS * HD])
    w_uv = at("w_uv", 131.25, [P, C_HEADS * HD])
    turn_st = at("turn_st", 144, [P, 2, T])
    relu_st = at("relu_st", 133.25, [P, 2, 512])
    score = at("score", 137.25, [P, 3 * P])
    top8 = at("top8", 138.75, [P, 8])
    gain_rows = at("gain_rows", 139, [NK + 1, P])
    gains = at("gains", 139.5, [P, NK + 1])
    relx = at("relx", 139.75, [BUCKETS + 1, 32])
    onehot = at("onehot", 140, [BUCKETS + 1, 2, 384])
    bias_rows = at("bias_rows", 200.5, [16, 2, 384])
    mg_hi = at("mg_hi", 160, [P, NK * T], FR)
    mg_lo = at("mg_lo", 176, [P, NK * T], FR)
    mtmp = at("mtmp", 192, [P, 2, 3, T])
    msum = at("msum", 198, [P, NRAW, T])
    x1 = at("x1", 96, [P, NT, D])
    gffn = at("gffn", 8, [P, D])
    subk = at("subk", 0, [P, 2 * PH, P])
    h2 = at("h2", 112, [P, NT, D])
    h2T = at("h2T", 128, [P, NK, T])
    sc = at("sc", 144, [P, NU * 2 * PKEYS])
    subkT = at("subkT", 192, [P, 2 * PH, P])
    u_ring = at("u_ring", 0, [P, RING, D])
    v_ring = at("v_ring", 32, [P, RING, D])
    junk = at("junk", 160, [P, D])
    gfin = at("gfin", 168, [P, D])
    diag = at("diag", 176, [P, RING, P])
    sc_w = at("sc_w", 178, [P, 2, PKEYS])
    sc_r = at("sc_r", 179, [P, 2, PKEYS])
    cand = at("cand", 180, [P, PTOP, PTOP])
    cand_r = at("cand_r", 181, [P, PTOP, PTOP])
    pick = at("pick", 182, [P, 2, PTOP, PTOP])
    idx_all = at("idx_all", 184, [P, NU * PTOP], U32)
    gw_all = at("gw_all", 185, [P, NU * PTOP])
    qp_st = at("qp_st", 186, [P, 2, T])
    iota16 = at("iota16", 188, [P, PTOP])
    tv = at("tv", 188.0625, [P, 2, PTOP])
    ti = at("ti", 188.1875, [P, 2, PTOP], U32)
    tif = at("tif", 188.3125, [P, 2, PTOP])
    ts = at("ts", 188.4375, [P, PTOP])
    tp = at("tp", 188.5, [P, PTOP], U32)
    thl = at("thl", 188.5625, [P, 2, PTOP], U32)
    thlf = at("thlf", 188.6875, [P, 2, PTOP])
    esel = at("esel", 188.8125, [P, 2, PTOP])
    eidx = at("eidx", 188.9375, [P, PTOP])
    texp = at("texp", 189, [P, PTOP])
    dots = at("dots", 189.0625, [P, 2, PTOP])
    gel = at("gel", 189.1875, [P, 2, PTOP])
    coef = at("coef", 189.3125, [P, 2, PTOP])
    stage_u = at("stage_u", 189.4375, [P, 2, PTOP], U32)
    stage_v = at("stage_v", 189.5625, [P, 2, PTOP], U32)
    iota_i = at("iota_i", 189.6875, [P, PTOP], mybir.dt.int32)
    tsum = at("tsum", 189.75, [P, 8])
    outst = at("outst", 64, [P, NT, D])
    ps = ctx.enter_context(nc.psum_tensor("ps", [P, 8, 512], F32))
    J, S_BANK, O_BANK, T_BANK, PT_BANK = 0, 2, 4, 5, 6
    bias_dram = nc.dram_tensor("bias_by_distance", (32, 384), F32, kind="Internal")
    onehot_dram = nc.inline_tensor(bucket_onehots(), name="bucket_onehots").ap()
    bias_d = bias_dram.ap()
    bias_full = nc.dram_tensor("bias_by_query", (32, P, T), F32, kind="Internal").ap()

    x_in = sem("x_in")
    const_in = sem("const_in")
    uk_in = sem("uk_in")
    raw_in = [sem(f"raw_in{i}") for i in range(NRAW)]
    ident_ok = sem("ident_ok")
    pads_ok = sem("pads_ok")
    relx_ok = sem("relx_ok")
    hi_done = sem("hi_done")
    lo_done = sem("lo_done")
    blk_done = sem("blk_done")
    evac_done = sem("evac_done")
    ssq_ok = sem("ssq_ok")
    ve_ok = sem("ve_ok")
    rt_ok = sem("rt_ok")
    xn_ok = sem("xn_ok")
    pre_pe = sem("pre_pe")
    pre_ev = sem("pre_ev")
    bias_out = sem("bias_out")
    bias_sk = sem("bias_sk")
    xt_pe = sem("xt_pe")
    xt_hi = sem("xt_hi")
    xt_lo = sem("xt_lo")
    cn_ok = sem("cn_ok")
    turn_pe = sem("turn_pe")
    turn_ev = sem("turn_ev")
    ct_pe = sem("ct_pe")
    ct_ev = sem("ct_ev")
    up_pe = sem("up_pe")
    up_ev = sem("up_ev")
    lg_pe = sem("lg_pe")
    lg_ev = sem("lg_ev")
    lg_use = sem("lg_use")
    score_ok = sem("score_ok")
    causal_ok = sem("causal_ok")
    mask_ok = sem("mask_ok")
    q_ready = sem("q_ready")
    s_done = sem("s_done")
    b_in = [sem(f"b_in{i}") for i in range(2)]
    cb_ok = sem("cb_ok")
    sm_pass = sem("sm_pass")
    g_pass = sem("g_pass")
    s_read = sem("s_read")
    nm_ok = sem("nm_ok")
    e_done = sem("e_done")
    pt_done = sem("pt_done")
    pt_ev = sem("pt_ev")
    pv_done = sem("pv_done")
    o_done = sem("o_done")
    ot_done = sem("ot_done")
    y_ev = sem("y_ev")
    y_hi = sem("y_hi")
    y_lo = sem("y_lo")
    m_mul = sem("m_mul")
    m_sum = sem("m_sum")
    m_hi = sem("m_hi")
    m_lo = sem("m_lo")
    x1_in = sem("x1_in")
    x1_ok = sem("x1_ok")
    sk_in = sem("sk_in")
    sk_pe = sem("sk_pe")
    sk_ev = sem("sk_ev")
    h2_ok = sem("h2_ok")
    ht_pe = sem("ht_pe")
    ht_ev = sem("ht_ev")
    iota_ok = sem("iota_ok")
    qp_ev = sem("qp_ev")
    s2_pe = sem("s2_pe")
    s2_ev = sem("s2_ev")
    top_ok = sem("top_ok")
    ex_ok = sem("ex_ok")
    idx_ok = sem("idx_ok")
    st_ok = sem("st_ok")
    u_in = [sem(f"u_in{i}") for i in range(RING)]
    v_in = [sem(f"v_in{i}") for i in range(RING)]
    dot_ok = sem("dot_ok")
    arg_ok = sem("arg_ok")
    th_ok = sem("th_ok")
    dg_ok = sem("dg_ok")
    acc_ok = sem("acc_ok")
    fin_in = sem("fin_in")
    o_ok = sem("o_ok")
    out_in = sem("out_in")

    w_in_v = w_in[0].rearrange("(k p) c -> p k c", p=P)
    br_v = [(w[0].rearrange("(k p) c -> p k c", p=P), k0, k1)
            for w, k0, k1 in ((w_br_a, 0, 8), (w_br_b, 8, 12), (w_br_c, 12, 16))]
    w_out_v = w_out[0].rearrange("(k p) c -> p k c", p=P)
    w_q_v = peer_w_q[0].rearrange("(k p) c -> p k c", p=P)
    x_v = x[0].rearrange("(t p) d -> p t d", p=P)
    out_v = out[0].rearrange("(t p) d -> p t d", p=P)
    u_tab, v_tab = peer_u[0], peer_v[0]

    def span(start, size):
        return slice(start, start + size) if isinstance(start, int) else bass.ds(start, size)

    def wait(eng, s, value):
        if not isinstance(value, int) or value > 0:
            eng.wait_ge(s, value)

    def gate_on(eng, s, value, passed):
        if isinstance(value, int):
            return wait(eng, s, value)
        eng.wait_ge(s, value)
        eng.sem_inc(passed, 1)

    def attention_bodies(eng, body):
        for kind, (first, bodies, _) in LOOPS.items():
            start = 0
            if first == 0:
                body(kind, 0, 0)
                start = 1
            with eng.Fori(start, bodies) as i:
                body(kind, i, i + first)

    def peeled(eng, count, body):
        body(0)
        with eng.Fori(1, count) as i:
            body(i)

    def landed(n0, j):
        if isinstance(n0, int):
            return W_INC * ((n0 + j) // NRAW + 1)
        return (W_INC // NRAW) * n0 + W_INC * (j // NRAW + 1)

    block = ctx.enter_context(nc.Block())

    @block.sync
    def _(sp):
        for t in range(NT):
            sp.dma_start(xin[:, t, :], x_v[:, t, :]).then_inc(x_in, 16)
        for n, c in enumerate(FIRST_COLS):
            wait(sp, lo_done, n - NRAW + 1)
            sp.dma_start(raw[:, n % NRAW], w_in_v[:, :, c:c + P]).then_inc(raw_in[n % NRAW], W_INC)

        def body(kind, i, b):
            qcol = LOOPS[kind][2]
            cols = [2 * P * i + qcol, 2 * P * i + (qcol + P)]
            cols += [2 * P * b + (g + P * par) for par in range(2) for g in (GA, GB, GC)]
            for j, c in enumerate(cols):
                sp.wait_ge(lo_done, 8 * b + (N_FIRST + j - NRAW + 1))
                sp.dma_start(raw[:, j % NRAW], w_in_v[:, :, span(c, P)]).then_inc(raw_in[j % NRAW], W_INC)
        attention_bodies(sp, body)

        def branch(i):
            for j in range(NRAW):
                sp.wait_ge(lo_done, NRAW * i + (N_BR + j - NRAW + 1))
                for v, k0, k1 in br_v:
                    sp.dma_start(raw[:, j, k0:k1], v[:, :, span(P * NRAW * i + P * j, P)]).then_inc(raw_in[j], W_INC // 3)
        peeled(sp, NK // NRAW, branch)

        def project(i):
            for j in range(NRAW):
                sp.wait_ge(lo_done, NRAW * i + (N_OUT + j - NRAW + 1))
                sp.dma_start(raw_wide[:, j], w_out_v[:, NRAW * j:NRAW * (j + 1), span(WIDE * i, WIDE)]).then_inc(raw_in[j], W_INC)
        project(0)
        sp.wait_ge(m_mul, NK)
        sp.dma_start(x1[:, :, :], x_v).then_inc(x1_in, 16)
        sp.dma_start(gffn[:, :], g_ffn.to_broadcast([P, D])).then_inc(x1_in, 16)
        sp.dma_start(subk[:, :, :], peer_sub_keys[0].rearrange("h s k d -> k (h s) d")).then_inc(sk_in, 16)
        with sp.Fori(1, NK // NRAW) as i:
            project(i)

        for j in range(NRAW):
            sp.wait_ge(lo_done, N_WQ + j - NRAW + 1)
            sp.dma_start(raw[:, j], w_q_v[:, :, P * j:P * j + P]).then_inc(raw_in[j], W_INC)
        with sp.Fori(1, NK // NRAW) as i:
            for j in range(NRAW):
                sp.wait_ge(blk_done, NRAW * i + (N_WQ + j - NRAW + 1))
                sp.dma_start(raw[:, j], w_q_v[:, :, bass.ds(P * NRAW * i + P * j, P)]).then_inc(raw_in[j], W_INC)
        sp.wait_ge(x1_ok, NWIDE)
        sp.dma_start(gfin[:, :], g_final.rearrange("(a d) -> a d", a=1).to_broadcast([P, D])).then_inc(fin_in, 16)
        for t in range(NT):
            sp.wait_ge(o_ok, t + 1)
            sp.dma_start(out_v[:, t, :], outst[:, t, :]).then_inc(out_in, 16)
        sp.wait_ge(out_in, 16 * NT)

    @block.gpsimd
    def _(pool):
        nc.gpsimd.memset(ident[:, :], 0.0).then_inc(ident_ok, 1)
        pool.wait_ge(ident_ok, 1)
        nc.gpsimd.affine_select(out=ident[:, :], in_=ident[:, :], compare_op=ALU.not_equal, fill=1.0, base=0,
                                pattern=[[-1, P]], channel_multiplier=1).then_inc(ident_ok, 1)

        def load_bias(g):
            pool.dma_start(bias_st[:, g % 2], bias_full[2 * g:2 * g + 2].rearrange("h p s -> p h s")).then_inc(b_in[g % 2], 16)

        def mask_bias(g):
            pool.wait_ge(b_in[g % 2], 16 * (g // 2 + 1))
            pool.wait_ge(s_read, g)
            m1 = dsa_mask[:, 0:T].unsqueeze(1).to_broadcast([P, 2, T])
            m0 = dsa_mask[:, T:3 * P].unsqueeze(1).to_broadcast([P, 2, P])
            nc.gpsimd.tensor_tensor(cbias[:, :, 0:T], bias_st[:, g % 2], m1, ALU.add).then_inc(cb_ok, 1)
            nc.gpsimd.tensor_tensor(cbias[:, :, T:3 * P], bias_st[:, g % 2, :, P:T], m0, ALU.add).then_inc(cb_ok, 1)

        pool.wait_ge(bias_out, 32)
        src = bass.AP(bias_d.tensor, P - 1, [[3 * P, 32], [-1, P], [1, T]])
        pool.dma_start(bias_full, src).then_inc(bias_sk, 16)
        pool.wait_ge(bias_sk, 16)
        for g in range(2):
            load_bias(g)
        pool.wait_ge(score_ok, 1)
        nc.gpsimd.affine_select(out=score[:, 0:T], in_=score[:, 0:T], compare_op=ALU.is_ge, fill=NEG, base=P,
                                pattern=[[-1, T]], channel_multiplier=1).then_inc(causal_ok, 1)
        nc.gpsimd.affine_select(out=score[:, T:3 * P], in_=score[:, T:3 * P], compare_op=ALU.is_ge, fill=NEG, base=0,
                                pattern=[[-1, P]], channel_multiplier=1).then_inc(causal_ok, 1)
        for g in range(2, PAIRS):
            pool.wait_ge(s_read, g - 1)
            load_bias(g)
            if g == 13:
                pool.wait_ge(mask_ok, 1)
            if g >= 13:
                mask_bias(g - 1)
        mask_bias(PAIRS - 1)

        def merge(i):
            for j in range(NRAW):
                m = NRAW * i + j
                wait(pool, m_lo, m - NRAW + 1)
                pool.wait_ge(m_mul, m + 1)
                nc.gpsimd.tensor_tensor(mtmp[:, j % 2, 0], mtmp[:, j % 2, 0], mtmp[:, j % 2, 1], ALU.add).then_inc(m_sum, 1)
                pool.wait_ge(m_sum, 2 * m + 1)
                nc.gpsimd.tensor_tensor(msum[:, j], mtmp[:, j % 2, 0], mtmp[:, j % 2, 2], ALU.add).then_inc(m_sum, 1)
        peeled(pool, NK // NRAW, merge)

        pool.wait_ge(x1_ok, NWIDE)
        nc.gpsimd.iota(iota_i[:, :], pattern=[[1, PTOP]], base=0, channel_multiplier=0).then_inc(iota_ok, 1)

        def phase(c, par, u_on=True, v_on=True):
            staged = 0
            if isinstance(c, int):
                staged = min(c, NU - 1) + 1 + max(0, c - LAG + 1)
            else:
                staged = 2 * c + (2 - LAG)
            if u_on:
                pool.wait_ge(idx_ok, c + 1)
                nc.gpsimd.tensor_copy(stage_u[:, par], idx_all[:, span(PTOP * c, PTOP)]).then_inc(st_ok, 1)
            if v_on:
                nc.gpsimd.tensor_copy(stage_v[:, par], idx_all[:, span(PTOP * c - PTOP * LAG, PTOP)]).then_inc(st_ok, 1)
            pool.wait_ge(st_ok, staged)
            for k in range(PTOP):
                if u_on:
                    gate_on(pool, dot_ok, PTOP * c + (k - RING + 1), g_pass)
                    pool.indirect_dma_start(u_ring[:, k % RING], None, u_tab,
                                            bass.IndirectOffsetOnAxis(ap=stage_u[:, par, k:k + 1], axis=0)).then_inc(u_in[k % RING], 16)
                if v_on:
                    gate_on(pool, acc_ok, PTOP * c + (k - RING + 1 - PTOP * LAG), g_pass)
                    pool.indirect_dma_start(v_ring[:, k % RING], None, v_tab,
                                            bass.IndirectOffsetOnAxis(ap=stage_v[:, par, k:k + 1], axis=0)).then_inc(v_in[k % RING], 16)

        for c in range(LAG):
            phase(c, c % 2, v_on=False)
        for c in range(LAG, LAG + 2):
            phase(c, c % 2)
        with pool.Fori((LAG + 2) // 2, NU // 2) as i:
            for par in range(2):
                phase(2 * i + par, par)
        for c in range(NU, NU + LAG):
            phase(c, c % 2, u_on=False)

    @block.scalar
    def _(act):
        act.dma_start(gain_rows[0:NK, :], g_mix[0].rearrange("(k p) -> k p", p=P)).then_inc(const_in, 16)
        act.dma_start(gain_rows[NK:NK + 1, :], c_lat_gain).then_inc(const_in, 16)
        act.dma_start(onehot[:, :, :], onehot_dram).then_inc(const_in, 16)
        act.dma_start(relx[0:BUCKETS, :], rel_bias).then_inc(const_in, 16)
        act.dma_start(sinkb[:, :], a_sinks.to_broadcast([P, A_HEADS])).then_inc(const_in, 16)
        act.dma_start(w_uk[:, :], c_w_uk[0].rearrange("c h d -> c (h d)")).then_inc(uk_in, 16)
        act.dma_start(w_uv[:, :], c_w_uv[0].rearrange("c h d -> c (h d)")).then_inc(uk_in, 16)

        def high(n0, j):
            wait(act, blk_done, n0 + (j - NHL + 1))
            act.wait_ge(raw_in[j % NRAW], landed(n0, j))
            nc.scalar.activation(w_hi[:, j % NHL], raw[:, j % NRAW], ACT.Copy).then_inc(hi_done, 1)

        def root(q, cols):
            act.wait_ge(ve_ok, q + 1)
            nc.scalar.activation(stat[:, q, 4:4 + cols], stat[:, q, 2:2 + cols], ACT.Sqrt).then_inc(rt_ok, 1)

        for t in range(NT):
            act.wait_ge(x_in, 16 * NT)
            wait(act, ssq_ok, t)
            nc.scalar.activation(junk0[:, :], xin[:, t], ACT.Square, accum_out=stat[:, t, 0:1]).then_inc(ssq_ok, 1)
        for t in range(NT):
            root(t, 1)
        high(0, 0)
        act.wait_ge(pre_pe, 1)
        nc.scalar.activation(gains[:, :], ps[:, 6, 0:NK + 1], ACT.Copy).then_inc(pre_ev, 1)
        act.wait_ge(pre_pe, 3)
        nc.scalar.activation(bias_rows[:, 0], ps[0:16, 7, 0:384], ACT.Copy, scale=1.0 / SCALE).then_inc(pre_ev, 1)
        nc.scalar.activation(bias_rows[:, 1], ps[0:16, 1, 0:384], ACT.Copy, scale=1.0 / SCALE).then_inc(pre_ev, 1)
        act.wait_ge(pre_ev, 3)
        act.dma_start(bias_d[0:16, :], bias_rows[:, 0]).then_inc(bias_out, 16)
        act.dma_start(bias_d[16:32, :], bias_rows[:, 1]).then_inc(bias_out, 16)
        for k in range(NK):
            act.wait_ge(xt_pe, k + 1)
            nc.scalar.activation(act_hi[:, k], ps[:, 2 + k % 4, 0:T], ACT.Copy, scale=gains[:, k:k + 1]).then_inc(xt_hi, 1)
        high(0, 1)

        def turned(n):
            r = TURNED.index(n)
            act.wait_ge(turn_pe, r + 1)
            rows = ps[:, PT_BANK + r % 2, 0:T].rearrange("p (t c) -> p t c", t=NT)
            if n == 0:
                nc.scalar.activation(clat[:, :, :], rows, ACT.Copy).then_inc(turn_ev, 1)
                act.wait_ge(turn_ev, 1)
                for t in range(NT):
                    i = nc.scalar.activation(junk0[:, P * t:P * t + P], clat[:, t], ACT.Square, accum_out=stat[:, 2, t:t + 1])
                i.then_inc(ssq_ok, 1)
                root(2, 2)
            else:
                c = P * (n - 6) if n < 8 else V_B + P * (n - 12)
                nc.scalar.activation(vals[:, :, c:c + P], rows, ACT.Copy).then_inc(turn_ev, 1)

        for n in range(N_FIRST):
            act.wait_ge(blk_done, n + 1)
            if n + 2 <= N_FIRST:
                high(0, n + 2)
            bank = ps[:, J + n % 2]
            if n in TURNED:
                r = TURNED.index(n)
                wait(act, turn_pe, r - 1)
                nc.scalar.activation(turn_st[:, r % 2], bank[:, 0:T], ACT.Copy).then_inc(evac_done, 1)
            elif n == 1:
                nc.scalar.activation(ikwT[:, :], bank[:, 0:T], ACT.Copy)
                for g in range(4):
                    i = nc.scalar.activation(ikz[32 * g:32 * g + 32, g], bank[0:IDX_DIM, 0:T], ACT.Copy)
                i.then_inc(evac_done, 1)
            elif n < 4:
                nc.scalar.activation(iqT[:, n - 2], bank[:, 0:T], ACT.Copy).then_inc(evac_done, 1)
            elif n < 6:
                for half in range(2):
                    kv = 2 * (n - 4) + half
                    for dst in range(2):
                        i = nc.scalar.activation(kT[64 * dst:64 * dst + 64, T * kv:T * kv + T],
                                                 bank[64 * half:64 * half + 64, 0:T], ACT.Copy)
                i.then_inc(evac_done, 1)
            else:
                c = T * (KT_B + n - 8)
                nc.scalar.activation(kT[:, c:c + T], bank[:, 0:T], ACT.Copy).then_inc(evac_done, 1)
            if n - 1 in TURNED:
                turned(n - 1)
            if n == 3:
                act.wait_ge(ct_pe, 1)
                nc.scalar.activation(cT[:, :], ps[:, T_BANK, 0:T], ACT.Copy, scale=gains[:, NK:NK + 1]).then_inc(ct_ev, 1)
                act.wait_ge(ct_pe, 2)
                nc.scalar.activation(iw[:, :, :], ps[:, O_BANK, 0:T].rearrange("p (t c) -> p t c", t=NT)[:, :, IDX_DIM:IDX_DIM + IDX_HEADS],
                                     ACT.Copy).then_inc(ct_ev, 1)
            if n == 4:
                for j in range(2):
                    act.wait_ge(up_pe, j + 1)
                    c = T * (KT_C + 2 * j)
                    nc.scalar.activation(kT[:, c:c + 2 * T], ps[:, 6 + j, :], ACT.Copy).then_inc(up_ev, 1)
                for t in range(NT):
                    act.wait_ge(up_pe, 3 + t)
                    nc.scalar.activation(vals[:, t, V_C:V_COLS], ps[:, 4 + t, :], ACT.Copy).then_inc(up_ev, 1)
            if 5 <= n < 11:
                unit = n - 5
                act.wait_ge(lg_pe, unit + 1)
                wait(act, lg_use, unit - 1)
                nc.scalar.activation(relu_st[:, unit % 2], ps[:, S_BANK + unit % 2, :], ACT.Relu, scale=IDX_SCALE).then_inc(lg_ev, 1)

        turned(N_FIRST - 1)

        def body(kind, i, b):
            n0 = 8 * b + N_FIRST

            def gate(j):
                act.wait_ge(blk_done, n0 + (j + 1))
                nc.scalar.activation(gates[:, span(6 * T * b + T * (j - 2), T)], ps[:, J + j % 2, 0:T], ACT.Exp,
                                     scale=-1.0).then_inc(evac_done, 1)

            def queries(par):
                act.wait_ge(blk_done, n0 + (par + 1))
                wait(act, s_done, 2 * b + (par - 1))
                nc.scalar.activation(q_st[0:64, par, 0], ps[0:64, J + par, 0:T], ACT.Copy).then_inc(q_ready, 1)
                nc.scalar.activation(q_st[64:P, par, 1], ps[64:P, J + par, 0:T], ACT.Copy).then_inc(evac_done, 1)

            def exps(par):
                act.wait_ge(nm_ok, 2 * b + (par + 1))
                for hh in range(2):
                    for t in range(NT):
                        cols = slice(T, 3 * P) if t == 0 else slice(0, T)
                        ins = nc.scalar.activation(probs[:, par, hh, cols], probs[:, par, hh, cols], ACT.Exp,
                                                   bias=smax[:, par, 1, t, hh:hh + 1], accum_out=rsum[:, par, t, hh:hh + 1])
                if kind == "a":
                    ins = nc.scalar.activation(esink[:, par], esink[:, par], ACT.Exp)
                ins.then_inc(e_done, 1)

            def probs_t(par):
                act.wait_ge(pt_done, 2 * b + (par + 1))
                wait(act, pv_done, 2 * b + par)
                nc.scalar.activation(pT[:, 0], ps[:, PT_BANK, 0:3 * P], ACT.Copy)
                nc.scalar.activation(pT[:, 1], ps[:, PT_BANK + 1, 0:3 * P], ACT.Copy).then_inc(pt_ev, 1)

            def outs_t(par):
                act.wait_ge(ot_done, 2 * b + (par + 1))
                nc.scalar.activation(yT[:, span(2 * T * b + T * par, T)], ps[:, T_BANK, 0:T], ACT.Copy).then_inc(y_ev, 1)

            def hi(j):
                high(n0, j)

            hi(1)
            hi(2)
            queries(0)
            hi(3)
            queries(1)
            exps(0)
            hi(4)
            gate(2)
            exps(1)
            hi(5)
            gate(3)
            probs_t(0)
            hi(6)
            gate(4)
            probs_t(1)
            hi(7)
            gate(5)
            outs_t(0)
            hi(8)
            gate(6)
            outs_t(1)
            gate(7)
        attention_bodies(act, body)

        high(N_BR, 1)
        act.wait_ge(blk_done, N_BR)
        act.wait_ge(y_ev, PAIRS)
        for c in range(4):
            nc.scalar.activation(act_hi[:, 4 * c:4 * c + 4], yT[:, 4 * T * c:4 * T * (c + 1)].rearrange("p (k t) -> p k t", t=T),
                                 ACT.Copy).then_inc(y_hi, 1)

        def merge(i):
            for j in range(NRAW):
                m = NRAW * i + j
                high(NRAW * i + N_BR, j + 2)
                act.wait_ge(m_sum, 2 * m + 2)
                nc.scalar.activation(mg_hi[:, span(T * m, T)], msum[:, j], ACT.Copy).then_inc(m_hi, 1)
        peeled(act, NK // NRAW, merge)

        with act.Fori(0, NK // NRAW - 1) as i:
            for j in range(NRAW):
                high(NRAW * i + N_OUT, j + 2)
        for j in range(2):
            high(N_WQ - NRAW, j + 2)

        for c in range(4):
            act.wait_ge(sk_pe, c + 1)
            nc.scalar.activation(subkT[:, 4 * c:4 * c + 4], ps[:, PT_BANK + c % 2, :].rearrange("p (m k) -> p m k", m=4),
                                 ACT.Copy).then_inc(sk_ev, 1)
        act.wait_ge(x1_ok, NWIDE)
        for t in range(NT):
            act.wait_ge(ssq_ok, 3 + t)
            nc.scalar.activation(junk[:, :], x1[:, t], ACT.Square, accum_out=stat[:, 3 + t, 0:1]).then_inc(ssq_ok, 1)
        for t in range(NT):
            root(3 + t, 1)
        for c in range(2 * NT * 2):
            t, kg = divmod(c, 4)
            act.wait_ge(ht_pe, c + 1)
            nc.scalar.activation(h2T[:, 4 * kg:4 * kg + 4, P * t:P * t + P], ps[:, 2 + c % 4, :].rearrange("p (k t) -> p k t", k=4),
                                 ACT.Copy).then_inc(ht_ev, 1)

        def exps_of(u):
            act.wait_ge(top_ok, u + 1)
            nc.scalar.activation(texp[:, :], texp[:, :], ACT.Exp, accum_out=tsum[:, 0:1]).then_inc(ex_ok, 1)

        def tanh_of(u):
            act.wait_ge(arg_ok, u + 1)
            nc.scalar.activation(gel[:, 1], gel[:, 0], ACT.Tanh, scale=math.sqrt(2.0 / math.pi)).then_inc(th_ok, 1)

        sc_by_tile = sc[:, :].rearrange("p (t r) -> p t r", t=NT)
        for w in range(2 * PH):
            act.wait_ge(blk_done, N_WQ + w + 1)
            wait(act, s2_pe, w - 1)
            nc.scalar.activation(qp_st[:, w % 2], ps[:, J + w % 2, 0:T], ACT.Copy).then_inc(qp_ev, 1)
            act.wait_ge(s2_pe, w + 1)
            nc.scalar.activation(sc_by_tile[:, :, PKEYS * w:PKEYS * w + PKEYS], ps[:, S_BANK + w % 2, 0:2 * PKEYS].rearrange("p (t k) -> p t k", t=NT),
                                 ACT.Copy).then_inc(s2_ev, 1)
            if w in (1, 3, 5):
                exps_of(w // 2)
        tanh_of(0)
        with act.Fori(LAG, NU - 1) as c:
            exps_of(c + 1)
            tanh_of(c - 1)

        def out_norm(t):
            act.wait_ge(acc_ok, PTOP * PH * (t + 1))
            nc.scalar.activation(outst[:, t], ps[:, 4 * t:4 * t + 4, :], ACT.Square, accum_out=stat[:, 5 + t, 0:1]).then_inc(ssq_ok, 1)
            root(5 + t, 1)

        out_norm(0)
        tanh_of(NU - 2)
        tanh_of(NU - 1)
        out_norm(1)

    @block.vector
    def _(dve):
        def mean_root(q, cols, count):
            s = stat[:, q]
            dve.wait_ge(ssq_ok, q + 1)
            nc.vector.tensor_scalar(s[:, 2:2 + cols], s[:, 0:cols], 1.0 / count, EPS, ALU.mult, ALU.add).then_inc(ve_ok, 1)
            dve.wait_ge(rt_ok, q + 1)
            nc.vector.reciprocal(s[:, 6:6 + cols], s[:, 4:4 + cols])
            dve.drain()
            nc.vector.tensor_tensor(s[:, 4:4 + cols], s[:, 6:6 + cols], s[:, 6:6 + cols], ALU.mult)
            dve.drain()
            nc.vector.tensor_tensor(s[:, 4:4 + cols], s[:, 4:4 + cols], s[:, 2:2 + cols], ALU.mult)
            dve.drain()
            nc.vector.tensor_scalar(s[:, 4:4 + cols], s[:, 4:4 + cols], -0.5, 1.5, ALU.mult, ALU.add)
            dve.drain()
            nc.vector.tensor_tensor(s[:, 6:6 + cols], s[:, 6:6 + cols], s[:, 4:4 + cols], ALU.mult)
            dve.drain()

        def low(n0, j):
            dve.wait_ge(hi_done, n0 + (j + 1))
            nc.vector.tensor_tensor(w_lo[:, j % NHL], raw[:, j % NRAW], w_hi[:, j % NHL].bitcast(F32), ALU.subtract).then_inc(lo_done, 1)

        nc.vector.memset(relx[BUCKETS:BUCKETS + 1, :], NEG).then_inc(relx_ok, 1)
        nc.vector.memset(ikz[:, :, :], 0.0).then_inc(pads_ok, 1)
        nc.vector.memset(q_st[:, :, :, :], 0.0).then_inc(pads_ok, 1)
        for t in range(NT):
            mean_root(t, 1, D)
            nc.vector.tensor_scalar(xin[:, t], xin[:, t], stat[:, t, 6:7], None, ALU.mult).then_inc(xn_ok, 1)
        low(0, 0)
        for k in range(NK):
            dve.wait_ge(xt_hi, k + 1)
            nc.vector.scalar_tensor_tensor(out=act_lo[:, k], in0=ps[:, 2 + k % 4, 0:T], scalar=gains[:, k:k + 1],
                                           in1=act_hi[:, k].bitcast(F32), op0=ALU.mult, op1=ALU.subtract).then_inc(xt_lo, 1)
        low(0, 1)

        def add_logits(unit):
            dve.wait_ge(lg_ev, unit + 1)
            t, heads, width, c0 = (0, range(4 * unit, 4 * unit + 4), P, T) if unit < 2 else (1, range(2 * unit - 4, 2 * unit - 2), T, 0)
            part = score[:, c0:c0 + width]
            for m, h in enumerate(heads):
                src = relu_st[:, unit % 2, width * m:width * m + width]
                if h == 0:
                    last = nc.vector.tensor_scalar(part, src, iw[:, t, h:h + 1], None, ALU.mult)
                else:
                    last = nc.vector.scalar_tensor_tensor(out=part, in0=src, scalar=iw[:, t, h:h + 1], in1=part, op0=ALU.mult, op1=ALU.add)
                if m == len(heads) - 1:
                    last.then_inc(lg_use, 1)
                dve.drain()

        def take8(t):
            part = score[:, 0:T] if t else score[:, T:3 * P]
            nc.vector.max(top8[:, :], part)
            dve.drain()
            nc.vector.match_replace(part, top8[:, :], part, TAKEN)
            dve.drain()

        rounds = [(t, r) for r in range(C_TOPK // 8) for t in range(NT)]
        per_block = {11: rounds[0:3], 12: rounds[3:6], 13: rounds[6:9], 14: rounds[9:12], 15: rounds[12:16]}
        for n in range(N_FIRST):
            if n + 2 <= N_FIRST:
                low(0, n + 2)
            if n == 1:
                mean_root(2, 2, LATENT)
                for t in range(NT):
                    nc.vector.tensor_scalar(clat[:, t], clat[:, t], stat[:, 2, 6 + t:7 + t], None, ALU.mult).then_inc(cn_ok, 1)
            if n == 5:
                dve.wait_ge(ct_ev, 2)
            if 5 <= n < 11:
                add_logits(n - 5)
            if n == 10:
                nc.vector.tensor_copy(top8[:, :], score[:, 0:8]).then_inc(score_ok, 1)
            if n == 11:
                dve.wait_ge(causal_ok, 2)
            for t, _ in per_block.get(n, ()):
                take8(t)
        nc.vector.tensor_scalar(dsa_mask[:, :], score[:, :], TAKEN / 2, NEG / SCALE, ALU.is_gt, ALU.mult).then_inc(mask_ok, 1)

        def body(kind, i, b):
            n0 = 8 * b + N_FIRST

            def softmax(par):
                dve.wait_ge(s_done, 2 * b + (par + 1))
                if kind == "c":
                    dve.wait_ge(cb_ok, 4 * b + (2 * par - 22))
                else:
                    dve.wait_ge(b_in[par], 16 * b + 16)
                gate_on(dve, pt_done, 2 * b + (par - 1), sm_pass)
                for hh in range(2):
                    for t in range(NT):
                        cols = slice(0, T) if t else slice(T, 3 * P)
                        if kind == "c":
                            bias = cbias[:, hh, cols]
                        else:
                            bias = bias_st[:, par, hh] if t else bias_st[:, par, hh, P:T]
                        last = nc.vector.tensor_tensor_reduce(out=probs[:, par, hh, cols], in0=ps[:, S_BANK + hh, cols], in1=bias,
                                                              scale=SCALE, scalar=TAKEN, op0=ALU.add, op1=ALU.max,
                                                              accum_out=smax[:, par, 0, t, hh:hh + 1])
                last.then_inc(s_read, 1)
                dve.drain()
                if kind == "a":
                    sinks = sinkb[:, span(4 * b + 2 * par, 2)]
                    for t in range(NT):
                        nc.vector.tensor_tensor(smax[:, par, 0, t], smax[:, par, 0, t], sinks, ALU.max)
                    dve.drain()
                last = nc.vector.tensor_scalar(smax[:, par, 1], smax[:, par, 0], -1.0, None, ALU.mult)
                if kind == "a":
                    dve.drain()
                    for t in range(NT):
                        last = nc.vector.tensor_tensor(esink[:, par, t], smax[:, par, 1, t], sinks, ALU.add)
                last.then_inc(nm_ok, 1)

            def outputs(par):
                dve.wait_ge(e_done, 2 * b + (par + 1))
                if kind == "a":
                    nc.vector.tensor_tensor(rsum[:, par], rsum[:, par], esink[:, par], ALU.add)
                    dve.drain()
                nc.vector.reciprocal(rsum[:, par], rsum[:, par])
                dve.drain()
                dve.wait_ge(pv_done, 2 * b + (par + 1))
                wait(dve, ot_done, 2 * b + par)
                nc.vector.tensor_tensor(o_st[:, :, :].rearrange("p t (h d) -> p t h d", h=2),
                                        ps[:, O_BANK, 0:2 * P].rearrange("p (t h d) -> p t h d", t=NT, h=2),
                                        rsum[:, par].unsqueeze(3).to_broadcast([P, NT, 2, HD]), ALU.mult).then_inc(o_done, 1)

            def sigmoid(par):
                dve.wait_ge(evac_done, n0 + (5 + 3 * par))
                g = gates[:, span(6 * T * b + 3 * T * par, 3 * T)]
                nc.vector.tensor_scalar(g, g, 1.0, None, ALU.add)
                dve.drain()
                nc.vector.reciprocal(g, g)

            low(n0, 1)
            low(n0, 2)
            low(n0, 3)
            softmax(0)
            low(n0, 4)
            softmax(1)
            low(n0, 5)
            low(n0, 6)
            outputs(0)
            low(n0, 7)
            outputs(1)
            sigmoid(0)
            low(n0, 8)
            sigmoid(1)
        attention_bodies(dve, body)

        low(N_BR, 1)
        for c in range(4):
            dve.wait_ge(y_hi, c + 1)
            nc.vector.tensor_tensor(act_lo[:, 4 * c:4 * c + 4], yT[:, 4 * T * c:4 * T * (c + 1)].rearrange("p (k t) -> p k t", t=T),
                                    act_hi[:, 4 * c:4 * c + 4].bitcast(F32), ALU.subtract).then_inc(y_lo, 1)

        def merge(i):
            for j in range(NRAW):
                m = NRAW * i + j
                dve.wait_ge(blk_done, m + (N_BR + 1))
                wait(dve, m_sum, 2 * m - 2)
                nc.vector.tensor_tensor(mtmp[:, j % 2, 0:2], ps[:, J + j % 2, :].rearrange("p (g t) -> p g t", g=2),
                                        gates[:, span(3 * T * m, 2 * T)].rearrange("p (g t) -> p g t", g=2), ALU.mult)
                nc.vector.tensor_tensor(mtmp[:, j % 2, 2], ps[:, S_BANK + j % 2, 0:T], gates[:, span(3 * T * m + 2 * T, T)],
                                        ALU.mult).then_inc(m_mul, 1)
                low(NRAW * i + N_BR, j + 2)
                dve.wait_ge(m_hi, m + 1)
                nc.vector.tensor_tensor(mg_lo[:, span(T * m, T)], msum[:, j], mg_hi[:, span(T * m, T)].bitcast(F32),
                                        ALU.subtract).then_inc(m_lo, 1)
        peeled(dve, NK // NRAW, merge)

        dve.wait_ge(x1_in, 32)

        for c in range(NWIDE):
            last_one = c == NWIDE - 1
            for j in range(2 if last_one else 3):
                low(NRAW * c + N_OUT, j + 2)
            dve.wait_ge(blk_done, NRAW * (c + 1) + N_OUT)
            cols = x1[:, :, WIDE * c:WIDE * (c + 1)]
            nc.vector.tensor_tensor(cols, cols, ps[:, 2 * (c % 2):2 * (c % 2) + 2, :], ALU.add).then_inc(x1_ok, 1)
            if not last_one:
                low(NRAW * c + N_OUT, 5)

        for t in range(NT):
            mean_root(3 + t, 1, D)
            nc.vector.scalar_tensor_tensor(out=h2[:, t], in0=x1[:, t], scalar=stat[:, 3 + t, 6:7], in1=gffn[:, :],
                                           op0=ALU.mult, op1=ALU.mult).then_inc(h2_ok, 1)
        dve.wait_ge(iota_ok, 1)
        nc.vector.tensor_copy(iota16[:, :], iota_i[:, :])

        def pick_experts(u):
            nc.vector.tensor_copy(sc_w[:, :, :], sc[:, span(2 * PKEYS * u, 2 * PKEYS)].rearrange("p (s k) -> p s k", s=2))
            dve.drain()
            for s in range(2):
                nc.vector.max(tv[:, s, 0:8], sc_w[:, s])
            dve.drain()
            for s in range(2):
                nc.vector.max_index(ti[:, s, 0:8], tv[:, s, 0:8], sc_w[:, s])
                nc.vector.match_replace(sc_r[:, s], tv[:, s, 0:8], sc_w[:, s], TAKEN)
            dve.drain()
            for s in range(2):
                nc.vector.max(tv[:, s, 8:16], sc_r[:, s])
            dve.drain()
            for s in range(2):
                nc.vector.max_index(ti[:, s, 8:16], tv[:, s, 8:16], sc_r[:, s])
            nc.vector.tensor_tensor(cand[:, :, :], tv[:, 0].unsqueeze(2).to_broadcast([P, PTOP, PTOP]),
                                    tv[:, 1].unsqueeze(1).to_broadcast([P, PTOP, PTOP]), ALU.add)
            dve.drain()
            flat, flat_r = cand[:, :, :].rearrange("p a b -> p (a b)"), cand_r[:, :, :].rearrange("p a b -> p (a b)")
            nc.vector.max(ts[:, 0:8], flat)
            nc.vector.tensor_copy(tif[:, :, :], ti[:, :, :])
            dve.drain()
            nc.vector.max_index(tp[:, 0:8], ts[:, 0:8], flat)
            nc.vector.match_replace(flat_r, ts[:, 0:8], flat, TAKEN)
            dve.drain()
            nc.vector.max(ts[:, 8:16], flat_r)
            dve.drain()
            nc.vector.max_index(tp[:, 8:16], ts[:, 8:16], flat_r)
            nc.vector.tensor_scalar(texp[:, :], ts[:, :], ts[:, 0:1], None, ALU.subtract).then_inc(top_ok, 1)
            dve.drain()
            nc.vector.tensor_scalar(thl[:, 0], tp[:, :], 4, None, ALU.logical_shift_right)
            nc.vector.tensor_scalar(thl[:, 1], tp[:, :], PTOP - 1, None, ALU.bitwise_and)
            dve.drain()
            nc.vector.tensor_copy(thlf[:, :, :], thl[:, :, :])
            dve.drain()
            for s in range(2):
                nc.vector.tensor_tensor(pick[:, s], thlf[:, s].unsqueeze(2).to_broadcast([P, PTOP, PTOP]),
                                        iota16[:, :].unsqueeze(1).to_broadcast([P, PTOP, PTOP]), ALU.is_equal)
            dve.drain()
            for s in range(2):
                nc.vector.tensor_tensor(pick[:, s], pick[:, s], tif[:, s].unsqueeze(1).to_broadcast([P, PTOP, PTOP]), ALU.mult)
            dve.drain()
            nc.vector.tensor_reduce(esel[:, :, :], pick[:, :, :, :], AX.X, ALU.add)
            dve.drain()
            nc.vector.scalar_tensor_tensor(out=eidx[:, :], in0=esel[:, 0], scalar=float(PKEYS), in1=esel[:, 1], op0=ALU.mult, op1=ALU.add)
            dve.drain()
            nc.vector.tensor_copy(idx_all[:, span(PTOP * u, PTOP)], eidx[:, :]).then_inc(idx_ok, 1)
            dve.wait_ge(ex_ok, u + 1)
            nc.vector.reciprocal(tsum[:, 1:2], tsum[:, 0:1])
            dve.drain()
            nc.vector.tensor_scalar(gw_all[:, span(PTOP * u, PTOP)], texp[:, :], tsum[:, 1:2], 0.5, ALU.mult, ALU.mult)

        def dot(u, par, tile, k):
            dve.wait_ge(u_in[k % RING], 16 * (PTOP // RING) * u + 16 * (k // RING + 1))
            nc.vector.tensor_tensor_reduce(out=u_ring[:, k % RING], in0=u_ring[:, k % RING], in1=h2[:, tile], scale=1.0, scalar=0.0,
                                           op0=ALU.mult, op1=ALU.add, accum_out=dots[:, par, k:k + 1]).then_inc(dot_ok, 1)

        def diagonal(u, par, k):
            wait(dve, acc_ok, PTOP * u + (k - RING + 1))
            nc.vector.tensor_scalar(diag[:, k % RING], ident[:, :], coef[:, par, k:k + 1], None, ALU.mult).then_inc(dg_ok, 1)

        def coefficients(u, par):
            d = dots[:, par]
            dve.drain()
            nc.vector.tensor_tensor(gel[:, 0], d, d, ALU.mult)
            dve.drain()
            nc.vector.tensor_scalar(gel[:, 0], gel[:, 0], 0.044715, 1.0, ALU.mult, ALU.add)
            dve.drain()
            nc.vector.tensor_tensor(gel[:, 0], gel[:, 0], d, ALU.mult).then_inc(arg_ok, 1)
            dve.wait_ge(th_ok, u + 1)
            nc.vector.scalar_tensor_tensor(out=coef[:, par], in0=gel[:, 1], scalar=1.0, in1=d, op0=ALU.add, op1=ALU.mult)
            dve.drain()
            nc.vector.tensor_tensor(coef[:, par], coef[:, par], gw_all[:, span(PTOP * u, PTOP)], ALU.mult)
            dve.drain()

        def phase(c, par, tile, top=True, dots_on=True, weights=True):
            if top:
                pick_experts(c + 1)
            for k in range(PTOP):
                if dots_on:
                    dot(c, par, tile, k)
                if not isinstance(c, int) or c >= LAG:
                    diagonal(c - LAG, par, k)
            if weights:
                coefficients(c - 1, 1 - par)

        def out_norm(t):
            dve.wait_ge(fin_in, 16)
            mean_root(5 + t, 1, D)
            nc.vector.scalar_tensor_tensor(out=outst[:, t], in0=ps[:, 4 * t:4 * t + 4, :].rearrange("p a b -> p (a b)"),
                                           scalar=stat[:, 5 + t, 6:7], in1=gfin[:, :], op0=ALU.mult, op1=ALU.mult).then_inc(o_ok, 1)

        dve.wait_ge(s2_ev, 2)
        dve.drain()
        pick_experts(0)
        dve.wait_ge(s2_ev, 4)
        phase(0, 0, 0, weights=False)
        dve.wait_ge(s2_ev, 6)
        phase(1, 1, 0)
        dve.wait_ge(s2_ev, 8)
        phase(2, 0, 0)
        dve.wait_ge(s2_ev, 2 * PH)
        phase(3, 1, 0)
        with dve.Fori(2, PH // 2) as i:
            for par in range(2):
                phase(2 * i + par, par, 0)
        with dve.Fori(PH // 2, NU // 2 - 1) as i:
            for par in range(2):
                phase(2 * i + par, par, 1)
        phase(NU - 2, 0, 1)
        out_norm(0)
        phase(NU - 1, 1, 1, top=False)
        phase(NU, 0, 1, top=False, dots_on=False)
        phase(NU + 1, 1, 1, top=False, dots_on=False, weights=False)
        out_norm(1)

    @block.tensor
    def _(pe):
        PRODUCTS = ((0, 0), (0, 1), (1, 0))
        w_parts, act_parts, mg_parts = (w_hi, w_lo), (act_hi, act_lo), (mg_hi, mg_lo)
        w_wide = [w[:, :, :, :].rearrange("p s (a b) c -> p s a (b c)", b=WIDE // P) for w in w_parts]

        def by_column(out_ap, slot, k0, k1, waits=None):
            for k in range(k0, k1):
                if waits is not None:
                    waits(k)
                for m, (wp, ap) in enumerate(PRODUCTS):
                    last = nc.tensor.matmul(out_ap, w_parts[wp][:, slot, k], act_parts[ap][:, k],
                                            start=(k == k0 and m == 0), stop=(k == k1 - 1 and m == 2))
            return last

        pe.wait_ge(ident_ok, 2)
        pe.wait_ge(const_in, 16 * 5)
        nc.tensor.transpose(ps[:, 6, 0:NK + 1], gain_rows[0:NK + 1, :], ident[0:NK + 1, 0:NK + 1]).then_inc(pre_pe, 1)
        pe.wait_ge(relx_ok, 1)
        nc.tensor.matmul(ps[0:16, 7, 0:384], relx[:, 0:16], onehot[:, 0], start=True, stop=True).then_inc(pre_pe, 1)
        nc.tensor.matmul(ps[0:16, 1, 0:384], relx[:, 16:32], onehot[:, 1], start=True, stop=True).then_inc(pre_pe, 1)
        pe.wait_ge(xn_ok, NT)
        for k in range(NK):
            wait(pe, xt_lo, k - 3)
            for t in range(NT):
                last = nc.tensor.transpose(ps[:, 2 + k % 4, P * t:P * t + P], xin[:, t, P * k:P * k + P], ident[:, :])
            last.then_inc(xt_pe, 1)
        pe.wait_ge(xt_lo, NK)
        pe.wait_ge(pre_ev, 3)

        def logits(unit):
            pe.wait_ge(evac_done, 4)
            wait(pe, lg_ev, unit - 1)
            t, heads, width = (0, range(4 * unit, 4 * unit + 4), P) if unit < 2 else (1, range(2 * unit - 4, 2 * unit - 2), T)
            for m, h in enumerate(heads):
                last = nc.tensor.matmul(ps[:, S_BANK + unit % 2, width * m:width * m + width], iqT[:, h // 4, P * t:P * t + P],
                                        ikz[:, h % 4, 0:width], start=True, stop=True)
            last.then_inc(lg_pe, 1)

        def turn(n):
            r = TURNED.index(n)
            pe.wait_ge(evac_done, n + 1)
            wait(pe, turn_ev, r - 1)
            if r == 1:
                pe.wait_ge(up_ev, 4)
            for t in range(NT):
                last = nc.tensor.transpose(ps[:, PT_BANK + r % 2, P * t:P * t + P], turn_st[:, r % 2, P * t:P * t + P], ident[:, :])
            last.then_inc(turn_pe, 1)

        for n in range(N_FIRST):
            pe.wait_ge(lo_done, n + 1)
            wait(pe, evac_done, n - 1)
            bank, slot = ps[:, J + n % 2], n % NHL
            by_column(bank[:, 0:T], slot, 0, NK).then_inc(blk_done, 1)
            if n - 1 in TURNED:
                turn(n - 1)
            if n == 3:
                pe.wait_ge(cn_ok, NT)
                for t in range(NT):
                    last = nc.tensor.transpose(ps[:, T_BANK, P * t:P * t + P], clat[:, t], ident[:, :])
                last.then_inc(ct_pe, 1)
                for t in range(NT):
                    last = nc.tensor.transpose(ps[:, O_BANK, P * t:P * t + P], ikwT[:, P * t:P * t + P], ident[:, :])
                last.then_inc(ct_pe, 1)
            if n == 4:
                pe.wait_ge(uk_in, 32)
                pe.wait_ge(ct_ev, 2)
                for j in range(2):
                    for m in range(2):
                        c = P * (2 * j + m)
                        last = nc.tensor.matmul(ps[:, 6 + j, T * m:T * m + T], w_uk[:, c:c + P], cT[:, :], start=True, stop=True)
                    last.then_inc(up_pe, 1)
                for t in range(NT):
                    nc.tensor.matmul(ps[:, 4 + t, :], cT[:, P * t:P * t + P], w_uv[:, :], start=True, stop=True).then_inc(up_pe, 1)
            if 5 <= n < 11:
                if n == 5:
                    pe.wait_ge(pads_ok, 2)
                logits(n - 5)
        turn(N_FIRST - 1)
        pe.wait_ge(lg_ev, 6)
        pe.wait_ge(turn_ev, len(TURNED))

        def body(kind, i, b):
            n0 = 8 * b + N_FIRST

            def weights(j):
                pe.wait_ge(lo_done, n0 + (j + 1))
                pe.wait_ge(evac_done, n0 + (j - 1))
                by_column(ps[:, J + j % 2, 0:T], j % NHL, 0, NK).then_inc(blk_done, 1)

            def scores(par):
                pe.wait_ge(q_ready, 2 * b + (par + 1))
                pe.wait_ge(evac_done, n0 + (par + 1))
                wait(pe, s_read, 2 * b + par)
                key = T * i if kind == "a" else 2 * T * i + T * ((KT_B if kind == "b" else KT_C) + par)
                for hh in range(2):
                    nc.tensor.matmul(ps[:, S_BANK + hh, 0:T], q_st[:, par, hh, P:T], kT[:, span(key, T)], start=True, stop=True)
                    last = nc.tensor.matmul(ps[:, S_BANK + hh, T:3 * P], q_st[:, par, hh, 0:P], kT[:, span(key, P)], start=True, stop=True)
                last.then_inc(s_done, 1)

            def turn_probs(par):
                pe.wait_ge(e_done, 2 * b + (par + 1))
                wait(pe, pt_ev, 2 * b + par)
                for hh in range(2):
                    for c in range(3):
                        last = nc.tensor.transpose(ps[:, PT_BANK + hh, P * c:P * c + P], probs[:, par, hh, P * c:P * c + P], ident[:, :])
                last.then_inc(pt_done, 1)

            def values(par):
                pe.wait_ge(pt_ev, 2 * b + (par + 1))
                wait(pe, o_done, 2 * b + par)
                for hh in range(2):
                    col = HD * i if kind == "a" else 2 * P * i + ((V_B if kind == "b" else V_C) + P * par + HD * hh)
                    nc.tensor.matmul(ps[:, O_BANK, HD * hh:HD * hh + HD], pT[:, hh, T:3 * P], vals[:, 0, span(col, HD)], start=True, stop=True)
                    for s in range(NT):
                        last = nc.tensor.matmul(ps[:, O_BANK, P + HD * hh:P + HD * hh + HD], pT[:, hh, P * s:P * s + P],
                                                vals[:, s, span(col, HD)], start=(s == 0), stop=(s == NT - 1))
                last.then_inc(pv_done, 1)

            def turn_outs(par):
                pe.wait_ge(o_done, 2 * b + (par + 1))
                wait(pe, y_ev, 2 * b + par)
                for t in range(NT):
                    last = nc.tensor.transpose(ps[:, T_BANK, P * t:P * t + P], o_st[:, t], ident[:, :])
                last.then_inc(ot_done, 1)

            weights(0)
            weights(1)
            scores(0)
            weights(2)
            scores(1)
            weights(3)
            turn_probs(0)
            weights(4)
            turn_probs(1)
            values(0)
            weights(5)
            values(1)
            turn_outs(0)
            weights(6)
            turn_outs(1)
            weights(7)
        attention_bodies(pe, body)

        pe.wait_ge(evac_done, N_BR)

        def merge(i):
            for j in range(NRAW):
                pe.wait_ge(lo_done, NRAW * i + (N_BR + j + 1))
                wait(pe, m_mul, NRAW * i + (j - 1))
                waits = None
                if isinstance(i, int) and j == 0:
                    waits = lambda k: pe.wait_ge(y_lo, k // 4 + 1)
                by_column(ps[:, J + j % 2, 0:T], j % NHL, 0, 8, waits)
                by_column(ps[:, J + j % 2, T:2 * T], j % NHL, 8, 12, waits)
                by_column(ps[:, S_BANK + j % 2, 0:T], j % NHL, 12, NK, waits).then_inc(blk_done, 1)
        peeled(pe, NK // NRAW, merge)
        pe.wait_ge(m_mul, NK)
        pe.wait_ge(m_lo, NK)

        for c in range(NWIDE):
            wait(pe, x1_ok, c - 1)
            for j in range(NRAW):
                pe.wait_ge(lo_done, NRAW * c + N_OUT + j + 1)
                for t in range(NT):
                    for kk in range(NRAW):
                        k = NRAW * j + kk
                        for m, (wp, ap) in enumerate(PRODUCTS):
                            last = nc.tensor.matmul(ps[:, 2 * (c % 2) + t, :], mg_parts[ap][:, T * k + P * t:T * k + P * t + P],
                                                    w_wide[wp][:, j % NHL, kk], start=(k == 0 and m == 0), stop=(k == NK - 1 and m == 2))
                last.then_inc(blk_done, 1)

        pe.wait_ge(sk_in, 16)
        for c in range(4):
            wait(pe, sk_ev, c - 1)
            for m in range(4):
                last = nc.tensor.transpose(ps[:, PT_BANK + c % 2, P * m:P * m + P], subk[:, 4 * c + m], ident[:, :])
            last.then_inc(sk_pe, 1)
        for c in range(2 * NT * 2):
            t, kg = divmod(c, 4)
            pe.wait_ge(h2_ok, t + 1)
            wait(pe, ht_ev, c - 3)
            for m in range(4):
                k = 4 * kg + m
                last = nc.tensor.transpose(ps[:, 2 + c % 4, P * m:P * m + P], h2[:, t, P * k:P * k + P], ident[:, :])
            last.then_inc(ht_pe, 1)
        pe.wait_ge(ht_ev, 2 * NT * 2)
        pe.wait_ge(sk_ev, 4)
        pe.wait_ge(x1_ok, NWIDE)

        def queries(i):
            for j in range(NRAW):
                w = NRAW * i + j
                pe.wait_ge(raw_in[j], landed(NRAW * i + N_WQ, j))
                wait(pe, qp_ev, NRAW * i + (j - 1))
                for k in range(NK):
                    last = nc.tensor.matmul(ps[:, J + j % 2, 0:T], raw[:, j, k], h2T[:, k], start=(k == 0), stop=(k == NK - 1))
                last.then_inc(blk_done, 1)
                pe.wait_ge(qp_ev, w + 1)
                wait(pe, s2_ev, NRAW * i + (j - 1))
                for t in range(NT):
                    last = nc.tensor.matmul(ps[:, S_BANK + j % 2, P * t:P * t + P], qp_st[:, j % 2, P * t:P * t + P],
                                            subkT[:, span(w, 1)], start=True, stop=True)
                last.then_inc(s2_pe, 1)
        peeled(pe, NK // NRAW, queries)
        pe.wait_ge(s2_ev, 2 * PH)

        def add_rows(u, t, last_u=False):
            for k in range(PTOP):
                pe.wait_ge(v_in[k % RING], 16 * (PTOP // RING) * u + 16 * (k // RING + 1))
                pe.wait_ge(dg_ok, PTOP * u + (k + 1))
                for c in range(4):
                    last = nc.tensor.matmul(ps[:, 4 * t + c, :], diag[:, k % RING], v_ring[:, k % RING, 512 * c:512 * c + 512],
                                            start=False, stop=(last_u and k == PTOP - 1))
                last.then_inc(acc_ok, 1)

        for t in range(NT):
            for c in range(4):
                nc.tensor.matmul(ps[:, 4 * t + c, :], ident[:, :], x1[:, t, 512 * c:512 * c + 512], start=True, stop=False)
            with pe.Fori(PH // 2 * t, PH // 2 * (t + 1) - 1) as i:
                for par in range(2):
                    add_rows(2 * i + par, t)
            add_rows(PH * (t + 1) - 2, t)
            add_rows(PH * (t + 1) - 1, t, last_u=True)


_INS = ["x", "rel_bias", "g_mix", "w_in", "a_sinks", "c_lat_gain", "c_w_uk", "c_w_uv", "w_br_a", "w_br_b", "w_br_c",
        "w_out", "g_ffn", "peer_w_q", "peer_sub_keys", "peer_u", "peer_v", "g_final"]


def kernel(**inputs):
    import numpy as _np
    import concourse.bacc as _bacc
    from concourse import mybir as _mybir
    from concourse.bass_utils import run_bass_kernel_spmd as _run

    nc = _bacc.Bacc("TRN2", target_bir_lowering=False, num_devices=1)
    arrays, args = {}, []
    for name in _INS:
        a = _np.ascontiguousarray(inputs[name])
        arrays[f"in_{name}"] = a
        args.append(nc.dram_tensor(f"in_{name}", a.shape, _mybir.dt.from_np(a.dtype), kind="ExternalInput").ap())
    args.append(nc.dram_tensor("out_0", (1, T, D), F32, kind="ExternalOutput").ap())
    build(nc, *args)
    r = _run(nc, [arrays], core_ids=[0])
    return r.results[0]["out_0"]
```

```python
import math
from contextlib import ExitStack

import numpy as np

import concourse.bass as bass
from concourse import mybir

F32 = mybir.dt.float32
FR = mybir.dt.float32r
U32 = mybir.dt.uint32
ALU = mybir.AluOpType
ACT = mybir.ActivationFunctionType
AX = mybir.AxisListType

P = 128
T, D = 256, 2048
NT = T // P
NK = D // P
HD = 64
A_HEADS, A_KV, B_HEADS, C_HEADS = 16, 4, 8, 8
A_WINDOW = 128
LATENT, IDX_HEADS, IDX_DIM = 128, 8, 32
C_TOPK = min(256, T // 4)
BUCKETS, MAX_DIST = 32, 2048
PH, PKEYS, PTOP = 8, 128, 16
EPS = 1e-6
NEG = -1e30
SCALE = HD ** -0.5
IDX_SCALE = (IDX_DIM ** -0.5) * (IDX_HEADS ** -0.5)
TAKEN = -3.0e38

QA = 0
KA = QA + A_HEADS * HD
VA = KA + A_KV * HD
QB = VA + A_KV * HD
KB = QB + B_HEADS * HD
VB = KB + B_HEADS * HD
QC = VB + B_HEADS * HD
CL = QC + C_HEADS * HD
IQ = CL + LATENT
IK = IQ + IDX_HEADS * IDX_DIM
GA = IK + IDX_DIM + IDX_HEADS
GB = GA + D
GC = GB + D

NRAW, NHL = 4, 2
FIRST_COLS = [CL, IK, IQ, IQ + P, KA, KA + P, VA, VA + P] + [KB + P * j for j in range(4)] + [VB + P * j for j in range(4)]
N_FIRST = len(FIRST_COLS)
PAIRS = 16
TURNED = [0, 6, 7, 12, 13, 14, 15]
WIDE = 512
NWIDE = D // WIDE
N_BR = N_FIRST + 4 * PAIRS
N_OUT = N_BR + NK
N_WQ = N_OUT + NK
LOOPS = {"a": (0, 4, QA), "b": (4, 2, QB), "c": (6, 2, QC)}
KT_B, KT_C = 4, 8
V_B, V_C = A_KV * HD, A_KV * HD + B_HEADS * HD
V_COLS = V_C + C_HEADS * HD
PICK_STEPS = 13
PICKS = PH * PTOP
GTOK = 4
GROUPS = P // GTOK
NWQ = 8
W_INC = 48
RING = 4
NU = NT * PH


def bucket_onehots():
    d = 255 - np.arange(384)
    exact = BUCKETS // 2
    far = np.maximum(d, exact).astype(np.float32)
    large = exact + (np.log(far / np.float32(exact)) / np.float32(math.log(MAX_DIST / exact)) * np.float32(BUCKETS - exact)).astype(np.int32)
    bucket = np.where(d < exact, np.maximum(d, 0), np.minimum(large, BUCKETS - 1))
    out = np.zeros((BUCKETS + 1, 2, 384), np.float32)
    for n, keep in enumerate([(d >= 0) & (d < A_WINDOW), d >= 0]):
        out[np.where(keep, bucket, BUCKETS), n, np.arange(384)] = 1.0
    return out


def build(nc, x, rel_bias, g_mix, w_in, a_sinks, c_lat_gain, c_w_uk, c_w_uv, w_br_a, w_br_b, w_br_c,
          w_out, g_ffn, peer_w_q, peer_sub_keys, peer_u, peer_v, g_final, out):
    ctx = ExitStack()
    K = 1024
    base = 16896

    def at(name, kib, shape, dt=F32):
        return nc.alloc_sbuf_tensor_at(name, shape, dt, offset=base + int(kib * K))

    def sem(name):
        return ctx.enter_context(nc.semaphore(name))

    act_hi = at("act_hi", 0, [P, NK, T], FR)
    act_lo = at("act_lo", 16, [P, NK, T], FR)
    w_hi = at("w_hi", 32, [P, NHL, NK, P], FR)
    w_lo = at("w_lo", 48, [P, NHL, NK, P], FR)
    raw = at("raw", 64, [P, NRAW, NK, P])
    raw_wide = raw[:, :, :, :].rearrange("p s (a b) c -> p s a (b c)", b=WIDE // P)
    gates = at("gates", 96, [P, PAIRS * 3 * T])
    yT = at("yT", 144, [P, NK * T])
    kT = at("kT", 160, [P, 12 * T])
    vals = at("vals", 172, [P, NT, V_COLS])
    q_st = at("q_st", 182, [P, 2, 2, T])
    bias_st = at("bias_st", 186, [P, 2, 2, T])
    cbias = at("cbias", 190, [P, 2, 3 * P])
    dsa_mask = at("dsa_mask", 193, [P, 3 * P])
    probs = at("probs", 194.5, [P, 2, 2, 3 * P])
    pT = at("pT", 200.5, [P, 2, 3 * P])
    o_st = at("o_st", 203.5, [P, NT, P])
    ident = at("ident", 204.5, [P, P])
    sinkb = at("sinkb", 205, [P, A_HEADS])
    stat = at("stat", 205.0625, [P, 7, 8])
    smax = at("smax", 205.3125, [P, 2, 2, NT, 2])
    rsum = at("rsum", 205.375, [P, 2, NT, 2])
    esink = at("esink", 205.40625, [P, 2, NT, 2])
    xin = at("xin", 96, [P, NT, D])
    junk0 = at("junk0", 112, [P, D])
    ikz = at("ikz", 120, [P, 4, T])
    iqT = at("iqT", 124, [P, 2, T])
    ikwT = at("ikwT", 126, [P, T])
    iw = at("iw", 127, [P, NT, IDX_HEADS])
    clat = at("clat", 127.25, [P, NT, P])
    cT = at("cT", 128.25, [P, T])
    w_uk = at("w_uk", 129.25, [P, C_HEADS * HD])
    w_uv = at("w_uv", 131.25, [P, C_HEADS * HD])
    turn_st = at("turn_st", 144, [P, 2, T])
    relu_st = at("relu_st", 133.25, [P, 2, 512])
    score = at("score", 137.25, [P, 3 * P])
    top8 = at("top8", 138.75, [P, 8])
    gain_rows = at("gain_rows", 139, [NK + 1, P])
    gains = at("gains", 139.5, [P, NK + 1])
    relx = at("relx", 139.75, [BUCKETS + 1, 32])
    onehot = at("onehot", 140, [BUCKETS + 1, 2, 384])
    bias_rows = at("bias_rows", 200.5, [16, 2, 384])
    mg_hi = at("mg_hi", 160, [P, NK * T], FR)
    mg_lo = at("mg_lo", 176, [P, NK * T], FR)
    mtmp = at("mtmp", 192, [P, 2, 3, T])
    msum = at("msum", 198, [P, NRAW, T])
    x1 = at("x1", 96, [P, NT, D])
    gffn = at("gffn", 8, [P, D])
    subk = at("subk", 0, [P, 2 * PH, P])
    ct = at("ct", 0, [P, PKEYS, T])
    h2T = at("h2T", 16, [P, NK, T])
    wq_raw = at("wq_raw", 32, [P, NWQ, NK, P])
    qp_st = at("qp_st", 0, [P, 2, T])
    subkT = at("subkT", 112, [P, 2 * PH, P])
    junk = at("junk", 120, [P, D])
    h2 = at("h2", 128, [P, NT, D])
    sc = at("sc", 144, [P, NU * 2 * PKEYS])
    u_ring = at("u_ring", 160, [P, RING, D])
    sc_w = at("sc_w", 192, [P, 2, PKEYS])
    sc_r = at("sc_r", 193, [P, 2, PKEYS])
    cand = at("cand", 194, [P, PTOP, PTOP])
    iota_i = at("iota_i", 194, [P, P], mybir.dt.int32)
    cand_r = at("cand_r", 195, [P, PTOP, PTOP])
    pick = at("pick", 196, [P, 2, PTOP, PTOP])
    idx_all = at("idx_all", 198, [P, NU * PTOP], U32)
    cw_all = at("cw_all", 199, [P, NU * PTOP])
    key_all = at("key_all", 200, [P, 2, NU * PTOP])
    tv = at("tv", 202.0625, [P, 2, PTOP])
    ti = at("ti", 202.1875, [P, 2, PTOP], U32)
    tif = at("tif", 202.3125, [P, 2, PTOP])
    ts = at("ts", 202.4375, [P, PTOP])
    tp = at("tp", 202.5, [P, PTOP], U32)
    thl = at("thl", 202.5625, [P, 2, PTOP], U32)
    thlf = at("thlf", 202.6875, [P, 2, PTOP])
    esel = at("esel", 202.8125, [P, 2, PTOP])
    eidx = at("eidx", 202.9375, [P, PTOP])
    texp = at("texp", 203, [P, PTOP])
    dots = at("dots", 203.0625, [P, 2, PTOP])
    gel = at("gel", 203.1875, [P, 2, PTOP])
    coef = at("coef", 203.3125, [P, 2, PTOP])
    stage_u = at("stage_u", 203.4375, [P, 2, PTOP], U32)
    tsum = at("tsum", 203.75, [P, 8])
    one_col = at("one_col", 203.875, [P, 1])
    one_root = at("one_root", 205.25, [P, 1])
    part = at("part", 205.4375, [P, NT, NWIDE])
    pickT = at("pickT", 205.46875, [P, 3, P])
    iota_f = at("iota_f", 206.96875, [P, P])
    ones = at("ones", 144, [P, 2, 2, GTOK, PKEYS])
    v_hi = at("v_hi", 128, [P, NHL, D], FR)
    v_lo = at("v_lo", 144, [P, NHL, D], FR)
    c_hi = at("c_hi", 192, [P, NHL, T], FR)
    c_lo = at("c_lo", 194, [P, NHL, T], FR)
    gfin = at("gfin", 196, [P, D])
    x1f = at("x1f", 0, [P, NT, D])
    outst = at("outst", 16, [P, NT, D])
    ps = ctx.enter_context(nc.psum_tensor("ps", [P, 8, 512], F32))
    J, S_BANK, O_BANK, T_BANK, PT_BANK = 0, 2, 4, 5, 6
    SK_BANK = 4
    bias_dram = nc.dram_tensor("bias_by_distance", (32, 384), F32, kind="Internal")
    onehot_dram = nc.inline_tensor(bucket_onehots(), name="bucket_onehots").ap()
    bias_d = bias_dram.ap()
    x1_d = nc.dram_tensor("x1_kept", (P, NT, D), F32, kind="Internal").ap()
    bias_full = nc.dram_tensor("bias_by_query", (32, P, T), F32, kind="Internal").ap()

    x_in = [sem(f"x_in{t}") for t in range(NT)]
    const_in = sem("const_in")
    sink_in = sem("sink_in")
    uk_in = sem("uk_in")
    raw_in = [sem(f"raw_in{i}") for i in range(NRAW)]
    wq_in = [sem(f"wq_in{i}") for i in range(NWQ)]
    ident_ok = sem("ident_ok")
    pads_ok = sem("pads_ok")
    relx_ok = sem("relx_ok")
    hi_done = sem("hi_done")
    lo_done = sem("lo_done")
    blk_done = sem("blk_done")
    evac_done = sem("evac_done")
    SSQ = {0: 1, 1: 2, 2: 3, 5: 4, 6: 5}
    sq_ok = sem("sq_ok")
    ssq_ok = sem("ssq_ok")
    ve_ok = sem("ve_ok")
    rt_ok = sem("rt_ok")
    xn_ok = sem("xn_ok")
    pre_pe = sem("pre_pe")
    pre_ev = sem("pre_ev")
    bias_out = sem("bias_out")
    bias_sk = sem("bias_sk")
    xt_pe = sem("xt_pe")
    xt_hi = sem("xt_hi")
    xt_lo = sem("xt_lo")
    cn_ok = sem("cn_ok")
    turn_pe = sem("turn_pe")
    turn_ev = sem("turn_ev")
    ct_pe = sem("ct_pe")
    ct_ev = sem("ct_ev")
    up_pe = sem("up_pe")
    up_ev = sem("up_ev")
    lg_pe = sem("lg_pe")
    lg_ev = sem("lg_ev")
    lg_use = sem("lg_use")
    score_ok = sem("score_ok")
    causal_ok = sem("causal_ok")
    mask_ok = sem("mask_ok")
    q_ready = sem("q_ready")
    s_done = sem("s_done")
    b_in = [sem(f"b_in{i}") for i in range(2)]
    cb_ok = sem("cb_ok")
    sm_pass = sem("sm_pass")
    g_pass = sem("g_pass")
    s_read = sem("s_read")
    nm_ok = sem("nm_ok")
    e_done = sem("e_done")
    pt_done = sem("pt_done")
    pt_ev = sem("pt_ev")
    pv_done = sem("pv_done")
    o_done = sem("o_done")
    ot_done = sem("ot_done")
    y_ev = sem("y_ev")
    y_hi = sem("y_hi")
    y_lo = sem("y_lo")
    m_mul = sem("m_mul")
    m_sum = sem("m_sum")
    m_hi = sem("m_hi")
    m_lo = sem("m_lo")
    x1_in = sem("x1_in")
    x1_ok = sem("x1_ok")
    sk_in = sem("sk_in")
    sk_pe = sem("sk_pe")
    sk_ev = sem("sk_ev")
    h2_ok = sem("h2_ok")
    ht_pe = sem("ht_pe")
    ht_ev = sem("ht_ev")
    iota_ok = sem("iota_ok")
    qp_ev = sem("qp_ev")
    hq_pe = sem("hq_pe")
    hq_ev = sem("hq_ev")
    s2_pe = sem("s2_pe")
    s2_ev = sem("s2_ev")
    sw_ok = sem("sw_ok")
    top_ok = sem("top_ok")
    ex_ok = sem("ex_ok")
    idx_ok = sem("idx_ok")
    st_ok = sem("st_ok")
    u_in = [sem(f"u_in{i}") for i in range(RING)]
    dot_ok = sem("dot_ok")
    arg_ok = sem("arg_ok")
    th_ok = sem("th_ok")
    cw_ok = sem("cw_ok")
    x1_out = sem("x1_out")
    pk_pe = sem("pk_pe")
    pk_ev = sem("pk_ev")
    ab_ok = sem("ab_ok")
    re_ok = sem("re_ok")
    oh_ok = sem("oh_ok")
    c_pe = sem("c_pe")
    c_ev = sem("c_ev")
    v_in = [sem(f"v_in{i}") for i in range(RING)]
    vh_ok = sem("vh_ok")
    vl_ok = sem("vl_ok")
    acc_ok = sem("acc_ok")
    fin_pe = sem("fin_pe")
    res_in = sem("res_in")
    sum_ok = sem("sum_ok")
    fin_in = sem("fin_in")
    o_ok = sem("o_ok")
    out_in = sem("out_in")

    w_in_v = w_in[0].rearrange("(k p) c -> p k c", p=P)
    br_v = [(w[0].rearrange("(k p) c -> p k c", p=P), k0, k1)
            for w, k0, k1 in ((w_br_a, 0, 8), (w_br_b, 8, 12), (w_br_c, 12, 16))]
    w_out_v = w_out[0].rearrange("(k p) c -> p k c", p=P)
    w_q_v = peer_w_q[0].rearrange("(k p) c -> p k c", p=P)
    x_v = x[0].rearrange("(t p) d -> p t d", p=P)
    out_v = out[0].rearrange("(t p) d -> p t d", p=P)
    u_tab, v_tab = peer_u[0], peer_v[0]

    def span(start, size):
        return slice(start, start + size) if isinstance(start, int) else bass.ds(start, size)

    def wait(eng, s, value):
        if not isinstance(value, int) or value > 0:
            eng.wait_ge(s, value)

    def gate_on(eng, s, value, passed):
        if isinstance(value, int):
            return wait(eng, s, value)
        eng.wait_ge(s, value)
        eng.sem_inc(passed, 1)

    def attention_bodies(eng, body):
        for kind, (first, bodies, _) in LOOPS.items():
            start = 0
            if first == 0:
                body(kind, 0, 0)
                start = 1
            with eng.Fori(start, bodies) as i:
                body(kind, i, i + first)

    def peeled(eng, count, body):
        body(0)
        with eng.Fori(1, count) as i:
            body(i)

    def landed(n0, j):
        if isinstance(n0, int):
            return W_INC * ((n0 + j) // NRAW + 1)
        return (W_INC // NRAW) * n0 + W_INC * (j // NRAW + 1)

    block = ctx.enter_context(nc.Block())

    @block.sync
    def _(sp):
        sp.dma_start(xin[:, 0, :], x_v[:, 0, :]).then_inc(x_in[0], 16)
        sp.dma_start(gain_rows[0:NK, :], g_mix[0].rearrange("(k p) -> k p", p=P)).then_inc(const_in, 16)
        sp.dma_start(gain_rows[NK:NK + 1, :], c_lat_gain).then_inc(const_in, 16)
        sp.dma_start(onehot[:, :, :], onehot_dram).then_inc(const_in, 16)
        sp.dma_start(relx[0:BUCKETS, :], rel_bias).then_inc(const_in, 16)
        sp.dma_start(xin[:, 1, :], x_v[:, 1, :]).then_inc(x_in[1], 16)
        for n, c in enumerate(FIRST_COLS):
            wait(sp, lo_done, n - NRAW + 1)
            sp.dma_start(raw[:, n % NRAW], w_in_v[:, :, c:c + P]).then_inc(raw_in[n % NRAW], W_INC)

        def body(kind, i, b):
            qcol = LOOPS[kind][2]
            cols = [2 * P * i + qcol, 2 * P * i + (qcol + P)]
            cols += [2 * P * b + (g + P * par) for par in range(2) for g in (GA, GB, GC)]
            for j, c in enumerate(cols):
                sp.wait_ge(lo_done, 8 * b + (N_FIRST + j - NRAW + 1))
                sp.dma_start(raw[:, j % NRAW], w_in_v[:, :, span(c, P)]).then_inc(raw_in[j % NRAW], W_INC)
        attention_bodies(sp, body)

        def branch(i):
            for j in range(NRAW):
                sp.wait_ge(lo_done, NRAW * i + (N_BR + j - NRAW + 1))
                for v, k0, k1 in br_v:
                    sp.dma_start(raw[:, j, k0:k1], v[:, :, span(P * NRAW * i + P * j, P)]).then_inc(raw_in[j], W_INC // 3)
        peeled(sp, NK // NRAW, branch)

        def project(i):
            for j in range(NRAW):
                sp.wait_ge(lo_done, NRAW * i + (N_OUT + j - NRAW + 1))
                sp.dma_start(raw_wide[:, j], w_out_v[:, NRAW * j:NRAW * (j + 1), span(WIDE * i, WIDE)]).then_inc(raw_in[j], W_INC)
        project(0)
        sp.wait_ge(m_mul, NK)
        sp.dma_start(x1[:, :, :], x_v).then_inc(x1_in, 16)
        sp.dma_start(gffn[:, :], g_ffn.to_broadcast([P, D])).then_inc(x1_in, 16)
        sp.dma_start(subk[:, :, :], peer_sub_keys[0].rearrange("h s k d -> k (h s) d")).then_inc(sk_in, 16)
        with sp.Fori(1, NK // NRAW) as i:
            project(i)

        def load_wq(w):
            sp.dma_start(wq_raw[:, (w + NWQ // 2) % NWQ], w_q_v[:, :, P * w:P * w + P]).then_inc(wq_in[w % NWQ], 16)

        for w in range(NRAW):
            sp.wait_ge(lo_done, N_WQ + w - NRAW + 1)
            load_wq(w)
        sp.wait_ge(x1_ok, NWIDE)
        for w in range(NRAW, NWQ):
            load_wq(w)
        sp.dma_start(x1_d, x1[:, :, :]).then_inc(x1_out, 16)
        for w in range(NWQ, 2 * PH):
            sp.wait_ge(blk_done, N_WQ + w - NWQ + 1)
            load_wq(w)

        v_blocks = v_tab.rearrange("(b p) d -> b p d", p=P)

        def load_v(n, slot):
            sp.dma_start(u_ring[:, slot], v_blocks[n] if isinstance(n, int) else v_blocks[bass.ds(n, 1)].rearrange("b p d -> (b p) d")).then_inc(v_in[slot], 16)

        for j in range(RING):
            sp.wait_ge(dot_ok, NU * PTOP - RING + 1 + j)
            load_v(j, j)

        def stream(i0, i1):
            with sp.Fori(i0, i1) as i:
                for j in range(RING):
                    sp.wait_ge(vl_ok, RING * i + (j - RING + 1))
                    load_v(RING * i + j, j)
        half = PKEYS // RING // 2
        stream(1, half)
        sp.wait_ge(vl_ok, RING * (half - 1))
        sp.dma_start(gfin[:, :], g_final.rearrange("(a d) -> a d", a=1).to_broadcast([P, D])).then_inc(fin_in, 16)
        sp.dma_start(x1f[:, :, :], x1_d).then_inc(res_in, 16)
        stream(half, PKEYS // RING)
        for t in range(NT):
            for h in range(2):
                cols = slice(D // 2 * h, D // 2 * (h + 1))
                sp.wait_ge(o_ok, 2 * t + h + 1)
                sp.dma_start(out_v[:, t, cols], outst[:, t, cols]).then_inc(out_in, 16)
        sp.wait_ge(out_in, 16 * 2 * NT)

    @block.gpsimd
    def _(pool):
        nc.gpsimd.memset(ident[:, :], 0.0).then_inc(ident_ok, 1)
        pool.wait_ge(ident_ok, 1)
        nc.gpsimd.affine_select(out=ident[:, :], in_=ident[:, :], compare_op=ALU.not_equal, fill=1.0, base=0,
                                pattern=[[-1, P]], channel_multiplier=1).then_inc(ident_ok, 1)

        def load_bias(g):
            pool.dma_start(bias_st[:, g % 2], bias_full[2 * g:2 * g + 2].rearrange("h p s -> p h s")).then_inc(b_in[g % 2], 16)

        def mask_bias(g):
            pool.wait_ge(b_in[g % 2], 16 * (g // 2 + 1))
            pool.wait_ge(s_read, g)
            m1 = dsa_mask[:, 0:T].unsqueeze(1).to_broadcast([P, 2, T])
            m0 = dsa_mask[:, T:3 * P].unsqueeze(1).to_broadcast([P, 2, P])
            nc.gpsimd.tensor_tensor(cbias[:, :, 0:T], bias_st[:, g % 2], m1, ALU.add).then_inc(cb_ok, 1)
            nc.gpsimd.tensor_tensor(cbias[:, :, T:3 * P], bias_st[:, g % 2, :, P:T], m0, ALU.add).then_inc(cb_ok, 1)

        pool.wait_ge(bias_out, 32)
        src = bass.AP(bias_d.tensor, P - 1, [[3 * P, 32], [-1, P], [1, T]])
        pool.dma_start(bias_full, src).then_inc(bias_sk, 16)
        pool.wait_ge(bias_sk, 16)
        for g in range(2):
            load_bias(g)
        pool.wait_ge(score_ok, 1)
        nc.gpsimd.affine_select(out=score[:, 0:T], in_=score[:, 0:T], compare_op=ALU.is_ge, fill=NEG, base=P,
                                pattern=[[-1, T]], channel_multiplier=1).then_inc(causal_ok, 1)
        nc.gpsimd.affine_select(out=score[:, T:3 * P], in_=score[:, T:3 * P], compare_op=ALU.is_ge, fill=NEG, base=0,
                                pattern=[[-1, P]], channel_multiplier=1).then_inc(causal_ok, 1)
        for g in range(2, PAIRS):
            pool.wait_ge(s_read, g - 1)
            load_bias(g)
            if g == 13:
                pool.wait_ge(mask_ok, 1)
            if g >= 13:
                mask_bias(g - 1)
        mask_bias(PAIRS - 1)

        def merge(i):
            for j in range(NRAW):
                m = NRAW * i + j
                wait(pool, m_lo, m - NRAW + 1)
                pool.wait_ge(m_mul, m + 1)
                nc.gpsimd.tensor_tensor(mtmp[:, j % 2, 0], mtmp[:, j % 2, 0], mtmp[:, j % 2, 1], ALU.add).then_inc(m_sum, 1)
                pool.wait_ge(m_sum, 2 * m + 1)
                nc.gpsimd.tensor_tensor(msum[:, j], mtmp[:, j % 2, 0], mtmp[:, j % 2, 2], ALU.add).then_inc(m_sum, 1)
        peeled(pool, NK // NRAW, merge)

        pool.wait_ge(x1_ok, NWIDE)
        nc.gpsimd.iota(iota_i[:, :], pattern=[[1, P]], base=0, channel_multiplier=0).then_inc(iota_ok, 1)

        def phase(c, par):
            pool.wait_ge(idx_ok, c + 1)
            nc.gpsimd.tensor_copy(stage_u[:, par], idx_all[:, span(PTOP * c, PTOP)]).then_inc(st_ok, 1)
            pool.wait_ge(st_ok, c + 1)
            for k in range(PTOP):
                gate_on(pool, dot_ok, PTOP * c + (k - RING + 1), g_pass)
                pool.indirect_dma_start(u_ring[:, k % RING], None, u_tab,
                                        bass.IndirectOffsetOnAxis(ap=stage_u[:, par, k:k + 1], axis=0)).then_inc(u_in[k % RING], 16)

        phase(0, 0)
        phase(1, 1)
        with pool.Fori(1, NU // 2) as i:
            for par in range(2):
                phase(2 * i + par, par)

    @block.scalar
    def _(act):
        act.dma_start(sinkb[:, :], a_sinks.to_broadcast([P, A_HEADS])).then_inc(sink_in, 16)
        act.dma_start(w_uk[:, :], c_w_uk[0].rearrange("c h d -> c (h d)")).then_inc(uk_in, 16)
        act.dma_start(w_uv[:, :], c_w_uv[0].rearrange("c h d -> c (h d)")).then_inc(uk_in, 16)

        def high(n0, j):
            wait(act, blk_done, n0 + (j - NHL + 1))
            act.wait_ge(raw_in[j % NRAW], landed(n0, j))
            nc.scalar.activation(w_hi[:, j % NHL], raw[:, j % NRAW], ACT.Copy).then_inc(hi_done, 1)

        def root(q, cols):
            act.wait_ge(ve_ok, q + 1)
            nc.scalar.activation(stat[:, q, 4:4 + cols], stat[:, q, 2:2 + cols], ACT.Sqrt).then_inc(rt_ok, 1)

        for t in range(NT):
            act.wait_ge(x_in[t], 16)
            wait(act, ssq_ok, t)
            nc.scalar.activation(junk0[:, :], xin[:, t], ACT.Square, accum_out=stat[:, t, 0:1]).then_inc(ssq_ok, 1)
            root(t, 1)
        high(0, 0)
        act.wait_ge(pre_pe, 1)
        nc.scalar.activation(gains[:, :], ps[:, 6, 0:NK + 1], ACT.Copy).then_inc(pre_ev, 1)
        act.wait_ge(pre_pe, 3)
        nc.scalar.activation(bias_rows[:, 0], ps[0:16, 7, 0:384], ACT.Copy, scale=1.0 / SCALE).then_inc(pre_ev, 1)
        nc.scalar.activation(bias_rows[:, 1], ps[0:16, 1, 0:384], ACT.Copy, scale=1.0 / SCALE).then_inc(pre_ev, 1)
        act.wait_ge(pre_ev, 3)
        act.dma_start(bias_d[0:16, :], bias_rows[:, 0]).then_inc(bias_out, 16)
        act.dma_start(bias_d[16:32, :], bias_rows[:, 1]).then_inc(bias_out, 16)
        for k in range(NK):
            act.wait_ge(xt_pe, k + 1)
            nc.scalar.activation(act_hi[:, k], ps[:, 2 + k % 4, 0:T], ACT.Copy, scale=gains[:, k:k + 1]).then_inc(xt_hi, 1)
        high(0, 1)

        def turned(n):
            r = TURNED.index(n)
            act.wait_ge(turn_pe, r + 1)
            rows = ps[:, PT_BANK + r % 2, 0:T].rearrange("p (t c) -> p t c", t=NT)
            if n == 0:
                nc.scalar.activation(clat[:, :, :], rows, ACT.Copy).then_inc(turn_ev, 1)
                act.wait_ge(turn_ev, 1)
                for t in range(NT):
                    i = nc.scalar.activation(junk0[:, P * t:P * t + P], clat[:, t], ACT.Square, accum_out=stat[:, 2, t:t + 1])
                i.then_inc(ssq_ok, 1)
                root(2, 2)
            else:
                c = P * (n - 6) if n < 8 else V_B + P * (n - 12)
                nc.scalar.activation(vals[:, :, c:c + P], rows, ACT.Copy).then_inc(turn_ev, 1)

        for n in range(N_FIRST):
            act.wait_ge(blk_done, n + 1)
            if n + 2 <= N_FIRST:
                high(0, n + 2)
            bank = ps[:, J + n % 2]
            if n in TURNED:
                r = TURNED.index(n)
                wait(act, turn_pe, r - 1)
                nc.scalar.activation(turn_st[:, r % 2], bank[:, 0:T], ACT.Copy).then_inc(evac_done, 1)
            elif n == 1:
                nc.scalar.activation(ikwT[:, :], bank[:, 0:T], ACT.Copy)
                for g in range(4):
                    i = nc.scalar.activation(ikz[32 * g:32 * g + 32, g], bank[0:IDX_DIM, 0:T], ACT.Copy)
                i.then_inc(evac_done, 1)
            elif n < 4:
                nc.scalar.activation(iqT[:, n - 2], bank[:, 0:T], ACT.Copy).then_inc(evac_done, 1)
            elif n < 6:
                for half in range(2):
                    kv = 2 * (n - 4) + half
                    for dst in range(2):
                        i = nc.scalar.activation(kT[64 * dst:64 * dst + 64, T * kv:T * kv + T],
                                                 bank[64 * half:64 * half + 64, 0:T], ACT.Copy)
                i.then_inc(evac_done, 1)
            else:
                c = T * (KT_B + n - 8)
                nc.scalar.activation(kT[:, c:c + T], bank[:, 0:T], ACT.Copy).then_inc(evac_done, 1)
            if n - 1 in TURNED:
                turned(n - 1)
            if n == 3:
                act.wait_ge(ct_pe, 1)
                nc.scalar.activation(cT[:, :], ps[:, T_BANK, 0:T], ACT.Copy, scale=gains[:, NK:NK + 1]).then_inc(ct_ev, 1)
                act.wait_ge(ct_pe, 2)
                nc.scalar.activation(iw[:, :, :], ps[:, O_BANK, 0:T].rearrange("p (t c) -> p t c", t=NT)[:, :, IDX_DIM:IDX_DIM + IDX_HEADS],
                                     ACT.Copy).then_inc(ct_ev, 1)
            if n == 4:
                for j in range(2):
                    act.wait_ge(up_pe, j + 1)
                    c = T * (KT_C + 2 * j)
                    nc.scalar.activation(kT[:, c:c + 2 * T], ps[:, 6 + j, :], ACT.Copy).then_inc(up_ev, 1)
                for t in range(NT):
                    act.wait_ge(up_pe, 3 + t)
                    nc.scalar.activation(vals[:, t, V_C:V_COLS], ps[:, 4 + t, :], ACT.Copy).then_inc(up_ev, 1)
            if 5 <= n < 11:
                unit = n - 5
                act.wait_ge(lg_pe, unit + 1)
                wait(act, lg_use, unit - 1)
                nc.scalar.activation(relu_st[:, unit % 2], ps[:, S_BANK + unit % 2, :], ACT.Relu, scale=IDX_SCALE).then_inc(lg_ev, 1)

        turned(N_FIRST - 1)

        def body(kind, i, b):
            n0 = 8 * b + N_FIRST

            def gate(j):
                act.wait_ge(blk_done, n0 + (j + 1))
                nc.scalar.activation(gates[:, span(6 * T * b + T * (j - 2), T)], ps[:, J + j % 2, 0:T], ACT.Tanh,
                                     scale=0.5).then_inc(evac_done, 1)

            def queries(par):
                act.wait_ge(blk_done, n0 + (par + 1))
                wait(act, s_done, 2 * b + (par - 1))
                nc.scalar.activation(q_st[0:64, par, 0], ps[0:64, J + par, 0:T], ACT.Copy).then_inc(q_ready, 1)
                nc.scalar.activation(q_st[64:P, par, 1], ps[64:P, J + par, 0:T], ACT.Copy).then_inc(evac_done, 1)

            def exps(par):
                act.wait_ge(nm_ok, 2 * b + (par + 1))
                for hh in range(2):
                    for t in range(NT):
                        cols = slice(T, 3 * P) if t == 0 else slice(0, T)
                        ins = nc.scalar.activation(probs[:, par, hh, cols], probs[:, par, hh, cols], ACT.Exp,
                                                   bias=smax[:, par, 1, t, hh:hh + 1], accum_out=rsum[:, par, t, hh:hh + 1])
                if kind == "a":
                    ins = nc.scalar.activation(esink[:, par], esink[:, par], ACT.Exp)
                ins.then_inc(e_done, 1)

            def probs_t(par):
                act.wait_ge(pt_done, 2 * b + (par + 1))
                wait(act, pv_done, 2 * b + par)
                nc.scalar.activation(pT[:, 0], ps[:, PT_BANK, 0:3 * P], ACT.Copy)
                nc.scalar.activation(pT[:, 1], ps[:, PT_BANK + 1, 0:3 * P], ACT.Copy).then_inc(pt_ev, 1)

            def outs_t(par):
                act.wait_ge(ot_done, 2 * b + (par + 1))
                nc.scalar.activation(yT[:, span(2 * T * b + T * par, T)], ps[:, T_BANK, 0:T], ACT.Copy).then_inc(y_ev, 1)

            def hi(j):
                high(n0, j)

            hi(1)
            hi(2)
            queries(0)
            hi(3)
            queries(1)
            exps(0)
            hi(4)
            gate(2)
            exps(1)
            hi(5)
            gate(3)
            probs_t(0)
            hi(6)
            gate(4)
            probs_t(1)
            hi(7)
            gate(5)
            outs_t(0)
            hi(8)
            gate(6)
            outs_t(1)
            gate(7)
        attention_bodies(act, body)

        act.wait_ge(blk_done, N_BR)
        act.wait_ge(y_ev, PAIRS)
        for c in range(4):
            nc.scalar.activation(act_hi[:, 4 * c:4 * c + 4], yT[:, 4 * T * c:4 * T * (c + 1)].rearrange("p (k t) -> p k t", t=T),
                                 ACT.Copy).then_inc(y_hi, 1)
        high(N_BR, 1)

        def merge(i):
            for j in range(NRAW):
                m = NRAW * i + j
                high(NRAW * i + N_BR, j + 2)
                act.wait_ge(m_sum, 2 * m + 2)
                nc.scalar.activation(mg_hi[:, span(T * m, T)], msum[:, j], ACT.Copy, scale=0.5).then_inc(m_hi, 1)
        peeled(act, NK // NRAW, merge)

        for c in range(NWIDE):
            for j in range(2 if c == NWIDE - 1 else NRAW):
                high(NRAW * c + N_OUT, j + 2)
            if c == NWIDE - 1:
                nc.scalar.activation(one_root[:, :], ident[:, 0:1], ACT.Sqrt)
            act.wait_ge(x1_ok, c + 1)
            for t in range(NT):
                wait(act, sq_ok, 2 * c + t - 1)
                last = nc.scalar.activation(junk[:, span(WIDE * (2 * (c % 2) + t), WIDE)], x1[:, t, WIDE * c:WIDE * (c + 1)], ACT.Square,
                                            accum_out=part[:, t, c:c + 1])
                last.then_inc(sq_ok, 1)
            if c == NWIDE - 2:
                for n in range(4):
                    act.wait_ge(sk_pe, n + 1)
                    nc.scalar.activation(subkT[:, 4 * n:4 * n + 4], ps[:, SK_BANK + n, :].rearrange("p (m k) -> p m k", m=4),
                                         ACT.Copy).then_inc(sk_ev, 1)
        for t in range(NT):
            root(3 + t, 1)
        def h2_turned(t):
            for kg in range(4):
                act.wait_ge(ht_pe, 4 * t + kg + 1)
                nc.scalar.activation(h2T[:, 4 * kg:4 * kg + 4, P * t:P * t + P], ps[:, SK_BANK + kg, :].rearrange("p (k t) -> p k t", k=4),
                                     ACT.Copy).then_inc(ht_ev, 1)
        h2_turned(0)

        def exps_of(u):
            act.wait_ge(top_ok, u + 1)
            nc.scalar.activation(texp[:, :], texp[:, :], ACT.Exp, accum_out=tsum[:, 0:1]).then_inc(ex_ok, 1)

        def scores_of(u):
            if isinstance(u, int) and u == 0:
                act.wait_ge(hq_ev, 4)
            else:
                act.wait_ge(s2_ev, 2 * u + 2 if isinstance(u, int) and u < PH else 2 * PH)
            wait(act, top_ok, u)
            nc.scalar.activation(sc_w[:, :, :], sc[:, span(2 * PKEYS * u, 2 * PKEYS)].rearrange("p (s k) -> p s k", s=2),
                                 ACT.Copy).then_inc(sw_ok, 1)

        def tanh_of(u):
            act.wait_ge(arg_ok, u + 1)
            nc.scalar.activation(gel[:, 1], gel[:, 0], ACT.Tanh, scale=math.sqrt(2.0 / math.pi)).then_inc(th_ok, 1)

        sc_by_tile = sc[:, :].rearrange("p (t r) -> p t r", t=NT)
        for w in range(2):
            act.wait_ge(hq_pe, w + 1)
            nc.scalar.activation(qp_st[:, w, 0:P], ps[:, J + w, 0:P], ACT.Copy).then_inc(hq_ev, 1)
        for w in range(2):
            act.wait_ge(hq_pe, 3 + w)
            nc.scalar.activation(sc[:, PKEYS * w:PKEYS * w + PKEYS], ps[:, S_BANK + w, 0:PKEYS], ACT.Copy).then_inc(hq_ev, 1)
        scores_of(0)
        h2_turned(1)
        for w in range(2 * PH):
            t0 = 1 if w < 2 else 0
            act.wait_ge(blk_done, N_WQ + w + 1)
            wait(act, s2_pe, w - 1)
            nc.scalar.activation(qp_st[:, w % 2, P * t0:T], ps[:, J + w % 2, P * t0:T], ACT.Copy).then_inc(qp_ev, 1)
            act.wait_ge(s2_pe, w + 1)
            nc.scalar.activation(sc_by_tile[:, t0:NT, PKEYS * w:PKEYS * w + PKEYS],
                                 ps[:, S_BANK + w % 2, PKEYS * t0:2 * PKEYS].rearrange("p (t k) -> p t k", t=NT - t0),
                                 ACT.Copy).then_inc(s2_ev, 1)
            if w == 1:
                exps_of(0)
            if w == 3:
                scores_of(1)
            if w == 5:
                exps_of(1)
                scores_of(2)
            if w == 8:
                tanh_of(0)
            if w == 12:
                exps_of(2)

        def picks_turned(tile):
            act.wait_ge(pk_pe, tile + 1)
            nc.scalar.activation(pickT[:, :, :], ps[:, 5, 0:3 * P].rearrange("p (a t) -> p a t", a=3), ACT.Copy).then_inc(pk_ev, 1)
            act.wait_ge(pk_ev, tile + 1)

        def one_hots(G, par, tok):
            wait(act, c_pe, G - 1)
            for key in range(2):
                for m in range(GTOK):
                    last = nc.scalar.activation(ones[:, key, par, m], iota_f[:, :], ACT.Abs, scale=-1.0, bias=pickT[:, key, span(tok + m, 1)])
            last.then_inc(ab_ok, 1)
            act.wait_ge(ab_ok, G + 1)
            nc.scalar.activation(ones[:, :, par], ones[:, :, par], ACT.Relu, scale=-1.0, bias=one_col[:, :]).then_inc(re_ok, 1)
            act.wait_ge(re_ok, G + 1)
            for m in range(GTOK):
                last = nc.scalar.activation(ones[:, 0, par, m], ones[:, 0, par, m], ACT.Copy, scale=pickT[:, 2, span(tok + m, 1)])
            last.then_inc(oh_ok, 1)

        def matrices(G, par, tok):
            act.wait_ge(c_pe, G + 1)
            nc.scalar.activation(ct[:, :, span(tok, GTOK)], ps[:, 6 + par].rearrange("p (t i) -> p i t", t=GTOK), ACT.Copy).then_inc(c_ev, 1)

        scores_of(3)
        with act.Fori(3, PH) as c:
            tanh_of(c - 2)
            exps_of(c)
            scores_of(c + 1)
        tanh_of(PH - 2)
        exps_of(PH)
        scores_of(PH + 1)
        act.wait_ge(x1_out, 16)

        def phase(c, picking=True, scoring=True):
            tanh_of(c - 1)
            if isinstance(c, int) and c == PH:
                picks_turned(0)
            for q in range(4):
                one_hots(GTOK * c + (q - GTOK * PH), q % 2, PTOP * c + (GTOK * q - PTOP * PH))
                matrices(GTOK * c + (q - GTOK * PH), q % 2, PTOP * c + (GTOK * q - PTOP * PH))
                if q == 1 and picking:
                    exps_of(c + 1)
                if q == 1 and scoring:
                    scores_of(c + 2)
        phase(PH)
        with act.Fori(PH + 1, NU - 2) as c:
            phase(c)
        phase(NU - 2, scoring=False)
        phase(NU - 1, picking=False, scoring=False)
        tanh_of(NU - 1)
        picks_turned(1)
        for j in range(NHL):
            act.wait_ge(v_in[j], 16)
            nc.scalar.activation(v_hi[:, j], u_ring[:, j], ACT.Copy)
        with act.Fori(0, GROUPS // 2) as i:
            for par in range(2):
                matrices(2 * i + (GROUPS + par), par, 2 * GTOK * i + (GTOK * par + P))
        act.wait_ge(c_ev, NT * GROUPS)

        def high_v(i):
            for j in range(RING):
                if not isinstance(i, int) or j >= NHL:
                    act.wait_ge(v_in[j], 16 * i + 16)
                    act.wait_ge(acc_ok, RING * i + (j - NHL + 1))
                    nc.scalar.activation(v_hi[:, j % NHL], u_ring[:, j], ACT.Copy)
                nc.scalar.activation(c_hi[:, j % NHL], ct[:, span(RING * i + j, 1)], ACT.Copy).then_inc(vh_ok, 1)
        peeled(act, PKEYS // RING, high_v)

        nc.scalar.activation(one_root[:, :], ident[:, 0:1], ACT.Sqrt)
        for t in range(NT):
            act.wait_ge(sum_ok, t + 1)
            nc.scalar.activation(outst[:, t], x1f[:, t], ACT.Square, accum_out=stat[:, 5 + t, 0:1]).then_inc(ssq_ok, 1)
            root(5 + t, 1)

    @block.vector
    def _(dve):
        def mean_root(q, cols, count, summed=False):
            s = stat[:, q]
            if not summed:
                dve.wait_ge(ssq_ok, SSQ[q])
            nc.vector.tensor_scalar(s[:, 2:2 + cols], s[:, 0:cols], 1.0 / count, EPS, ALU.mult, ALU.add).then_inc(ve_ok, 1)
            dve.wait_ge(rt_ok, q + 1)
            nc.vector.reciprocal(s[:, 6:6 + cols], s[:, 4:4 + cols])
            dve.drain()
            nc.vector.tensor_tensor(s[:, 4:4 + cols], s[:, 6:6 + cols], s[:, 6:6 + cols], ALU.mult)
            dve.drain()
            nc.vector.tensor_tensor(s[:, 4:4 + cols], s[:, 4:4 + cols], s[:, 2:2 + cols], ALU.mult)
            dve.drain()
            nc.vector.tensor_scalar(s[:, 4:4 + cols], s[:, 4:4 + cols], -0.5, 1.5, ALU.mult, ALU.add)
            dve.drain()
            nc.vector.tensor_tensor(s[:, 6:6 + cols], s[:, 6:6 + cols], s[:, 4:4 + cols], ALU.mult)
            dve.drain()

        def low(n0, j):
            dve.wait_ge(hi_done, n0 + (j + 1))
            nc.vector.tensor_tensor(w_lo[:, j % NHL], raw[:, j % NRAW], w_hi[:, j % NHL].bitcast(F32), ALU.subtract).then_inc(lo_done, 1)

        nc.vector.memset(relx[BUCKETS:BUCKETS + 1, :], NEG).then_inc(relx_ok, 1)
        nc.vector.memset(ikz[:, :, :], 0.0).then_inc(pads_ok, 1)
        nc.vector.memset(q_st[:, :, :, :], 0.0).then_inc(pads_ok, 1)
        for t in range(NT):
            mean_root(t, 1, D)
            nc.vector.tensor_scalar(xin[:, t], xin[:, t], stat[:, t, 6:7], None, ALU.mult).then_inc(xn_ok, 1)
        low(0, 0)
        for k in range(NK):
            dve.wait_ge(xt_hi, k + 1)
            nc.vector.scalar_tensor_tensor(out=act_lo[:, k], in0=ps[:, 2 + k % 4, 0:T], scalar=gains[:, k:k + 1],
                                           in1=act_hi[:, k].bitcast(F32), op0=ALU.mult, op1=ALU.subtract).then_inc(xt_lo, 1)
        low(0, 1)

        def add_logits(unit):
            dve.wait_ge(lg_ev, unit + 1)
            t, heads, width, c0 = (0, range(4 * unit, 4 * unit + 4), P, T) if unit < 2 else (1, range(2 * unit - 4, 2 * unit - 2), T, 0)
            part = score[:, c0:c0 + width]
            for m, h in enumerate(heads):
                src = relu_st[:, unit % 2, width * m:width * m + width]
                if h == 0:
                    last = nc.vector.tensor_scalar(part, src, iw[:, t, h:h + 1], None, ALU.mult)
                else:
                    last = nc.vector.scalar_tensor_tensor(out=part, in0=src, scalar=iw[:, t, h:h + 1], in1=part, op0=ALU.mult, op1=ALU.add)
                if m == len(heads) - 1:
                    last.then_inc(lg_use, 1)
                dve.drain()

        def take8(t):
            part = score[:, 0:T] if t else score[:, T:3 * P]
            nc.vector.max(top8[:, :], part)
            dve.drain()
            nc.vector.match_replace(part, top8[:, :], part, TAKEN)
            dve.drain()

        rounds = [(t, r) for r in range(C_TOPK // 8) for t in range(NT)]
        per_block = {11: rounds[0:3], 12: rounds[3:6], 13: rounds[6:9], 14: rounds[9:12], 15: rounds[12:16]}
        for n in range(N_FIRST):
            if n + 2 <= N_FIRST:
                low(0, n + 2)
            if n == 1:
                mean_root(2, 2, LATENT)
                for t in range(NT):
                    nc.vector.tensor_scalar(clat[:, t], clat[:, t], stat[:, 2, 6 + t:7 + t], None, ALU.mult).then_inc(cn_ok, 1)
            if n == 5:
                dve.wait_ge(ct_ev, 2)
            if 5 <= n < 11:
                add_logits(n - 5)
            if n == 10:
                nc.vector.tensor_copy(top8[:, :], score[:, 0:8]).then_inc(score_ok, 1)
            if n == 11:
                dve.wait_ge(causal_ok, 2)
            for t, _ in per_block.get(n, ()):
                take8(t)
        nc.vector.tensor_scalar(dsa_mask[:, :], score[:, :], TAKEN / 2, NEG / SCALE, ALU.is_gt, ALU.mult).then_inc(mask_ok, 1)

        def body(kind, i, b):
            n0 = 8 * b + N_FIRST

            def softmax(par):
                dve.wait_ge(s_done, 2 * b + (par + 1))
                if kind == "c":
                    dve.wait_ge(cb_ok, 4 * b + (2 * par - 22))
                else:
                    dve.wait_ge(b_in[par], 16 * b + 16)
                gate_on(dve, pt_done, 2 * b + (par - 1), sm_pass)
                for hh in range(2):
                    for t in range(NT):
                        cols = slice(0, T) if t else slice(T, 3 * P)
                        if kind == "c":
                            bias = cbias[:, hh, cols]
                        else:
                            bias = bias_st[:, par, hh] if t else bias_st[:, par, hh, P:T]
                        last = nc.vector.tensor_tensor_reduce(out=probs[:, par, hh, cols], in0=ps[:, S_BANK + hh, cols], in1=bias,
                                                              scale=SCALE, scalar=TAKEN, op0=ALU.add, op1=ALU.max,
                                                              accum_out=smax[:, par, 0, t, hh:hh + 1])
                last.then_inc(s_read, 1)
                dve.drain()
                if kind == "a":
                    sinks = sinkb[:, span(4 * b + 2 * par, 2)]
                    for t in range(NT):
                        nc.vector.tensor_tensor(smax[:, par, 0, t], smax[:, par, 0, t], sinks, ALU.max)
                    dve.drain()
                last = nc.vector.tensor_scalar(smax[:, par, 1], smax[:, par, 0], -1.0, None, ALU.mult)
                if kind == "a":
                    dve.drain()
                    for t in range(NT):
                        last = nc.vector.tensor_tensor(esink[:, par, t], smax[:, par, 1, t], sinks, ALU.add)
                last.then_inc(nm_ok, 1)

            def outputs(par):
                dve.wait_ge(e_done, 2 * b + (par + 1))
                if kind == "a":
                    nc.vector.tensor_tensor(rsum[:, par], rsum[:, par], esink[:, par], ALU.add)
                    dve.drain()
                nc.vector.reciprocal(rsum[:, par], rsum[:, par])
                dve.drain()
                dve.wait_ge(pv_done, 2 * b + (par + 1))
                wait(dve, ot_done, 2 * b + par)
                nc.vector.tensor_tensor(o_st[:, :, :].rearrange("p t (h d) -> p t h d", h=2),
                                        ps[:, O_BANK, 0:2 * P].rearrange("p (t h d) -> p t h d", t=NT, h=2),
                                        rsum[:, par].unsqueeze(3).to_broadcast([P, NT, 2, HD]), ALU.mult).then_inc(o_done, 1)

            low(n0, 1)
            low(n0, 2)
            low(n0, 3)
            softmax(0)
            low(n0, 4)
            softmax(1)
            low(n0, 5)
            low(n0, 6)
            outputs(0)
            low(n0, 7)
            outputs(1)
            low(n0, 8)
        dve.wait_ge(sink_in, 16)
        attention_bodies(dve, body)

        for c in range(4):
            dve.wait_ge(y_hi, c + 1)
            nc.vector.tensor_tensor(act_lo[:, 4 * c:4 * c + 4], yT[:, 4 * T * c:4 * T * (c + 1)].rearrange("p (k t) -> p k t", t=T),
                                    act_hi[:, 4 * c:4 * c + 4].bitcast(F32), ALU.subtract).then_inc(y_lo, 1)
        low(N_BR, 1)

        def merge(i):
            for j in range(NRAW):
                m = NRAW * i + j
                dve.wait_ge(blk_done, m + (N_BR + 1))
                wait(dve, m_sum, 2 * m - 2)
                nc.vector.scalar_tensor_tensor(out=mtmp[:, j % 2, 0:2].rearrange("p g t -> p (g t)"), in0=gates[:, span(3 * T * m, 2 * T)],
                                               scalar=1.0, in1=ps[:, J + j % 2, :], op0=ALU.add, op1=ALU.mult)
                nc.vector.scalar_tensor_tensor(out=mtmp[:, j % 2, 2], in0=gates[:, span(3 * T * m + 2 * T, T)], scalar=1.0,
                                               in1=ps[:, S_BANK + j % 2, 0:T], op0=ALU.add, op1=ALU.mult).then_inc(m_mul, 1)
                low(NRAW * i + N_BR, j + 2)
                dve.wait_ge(m_hi, m + 1)
                nc.vector.scalar_tensor_tensor(out=mg_lo[:, span(T * m, T)], in0=msum[:, j], scalar=0.5,
                                               in1=mg_hi[:, span(T * m, T)].bitcast(F32), op0=ALU.mult, op1=ALU.subtract).then_inc(m_lo, 1)
        peeled(dve, NK // NRAW, merge)


        for c in range(NWIDE):
            last_one = c == NWIDE - 1
            for j in range(2 if last_one else 3):
                low(NRAW * c + N_OUT, j + 2)
            dve.wait_ge(blk_done, NRAW * (c + 1) + N_OUT)
            if c == 0:
                dve.wait_ge(x1_in, 32)
            cols = x1[:, :, WIDE * c:WIDE * (c + 1)]
            nc.vector.tensor_tensor(cols, cols, ps[:, 2 * (c % 2):2 * (c % 2) + 2, :], ALU.add).then_inc(x1_ok, 1)
            if not last_one:
                low(NRAW * c + N_OUT, 5)

        dve.wait_ge(sq_ok, 2 * NWIDE)
        for t in range(NT):
            nc.vector.tensor_reduce(stat[:, 3 + t, 0:1], part[:, t, :], AX.X, ALU.add)
        dve.drain()
        for t in range(NT):
            mean_root(3 + t, 1, D, summed=True)
            nc.vector.scalar_tensor_tensor(out=h2[:, t], in0=x1[:, t], scalar=stat[:, 3 + t, 6:7], in1=gffn[:, :],
                                           op0=ALU.mult, op1=ALU.mult).then_inc(h2_ok, 1)
        dve.wait_ge(iota_ok, 1)
        nc.vector.tensor_copy(iota_f[:, :], iota_i[:, :])
        nc.vector.memset(one_col[:, :], 1.0)

        def pick_step(u, step):
            flat, flat_r = cand[:, :, :].rearrange("p a b -> p (a b)"), cand_r[:, :, :].rearrange("p a b -> p (a b)")
            if step == 0:
                gate_on(dve, sw_ok, u + 1, sm_pass)
            dve.drain()
            if step == 0:
                for s in range(2):
                    nc.vector.max(tv[:, s, 0:8], sc_w[:, s])
            elif step == 1:
                for s in range(2):
                    nc.vector.max_index(ti[:, s, 0:8], tv[:, s, 0:8], sc_w[:, s])
                    nc.vector.match_replace(sc_r[:, s], tv[:, s, 0:8], sc_w[:, s], TAKEN)
            elif step == 2:
                for s in range(2):
                    nc.vector.max(tv[:, s, 8:16], sc_r[:, s])
            elif step == 3:
                for s in range(2):
                    nc.vector.max_index(ti[:, s, 8:16], tv[:, s, 8:16], sc_r[:, s])
                nc.vector.tensor_tensor(cand[:, :, :], tv[:, 0].unsqueeze(2).to_broadcast([P, PTOP, PTOP]),
                                        tv[:, 1].unsqueeze(1).to_broadcast([P, PTOP, PTOP]), ALU.add)
            elif step == 4:
                nc.vector.max(ts[:, 0:8], flat)
                nc.vector.tensor_copy(tif[:, :, :], ti[:, :, :])
            elif step == 5:
                nc.vector.max_index(tp[:, 0:8], ts[:, 0:8], flat)
                nc.vector.match_replace(flat_r, ts[:, 0:8], flat, TAKEN)
            elif step == 6:
                nc.vector.max(ts[:, 8:16], flat_r)
            elif step == 7:
                nc.vector.max_index(tp[:, 8:16], ts[:, 8:16], flat_r)
                nc.vector.tensor_scalar(texp[:, :], ts[:, :], ts[:, 0:1], None, ALU.subtract).then_inc(top_ok, 1)
            elif step == 8:
                nc.vector.tensor_scalar(thl[:, 0], tp[:, :], 4, None, ALU.logical_shift_right)
                nc.vector.tensor_scalar(thl[:, 1], tp[:, :], PTOP - 1, None, ALU.bitwise_and)
                dve.drain()
                nc.vector.tensor_copy(thlf[:, :, :], thl[:, :, :])
            elif step == 9:
                for s in range(2):
                    nc.vector.tensor_tensor(pick[:, s], thlf[:, s].unsqueeze(2).to_broadcast([P, PTOP, PTOP]),
                                            iota_f[:, 0:PTOP].unsqueeze(1).to_broadcast([P, PTOP, PTOP]), ALU.is_equal)
                dve.drain()
                for s in range(2):
                    nc.vector.tensor_tensor(pick[:, s], pick[:, s], tif[:, s].unsqueeze(1).to_broadcast([P, PTOP, PTOP]), ALU.mult)
            elif step == 10:
                nc.vector.tensor_reduce(esel[:, :, :], pick[:, :, :, :], AX.X, ALU.add)
                dve.drain()
                nc.vector.scalar_tensor_tensor(out=eidx[:, :], in0=esel[:, 0], scalar=float(PKEYS), in1=esel[:, 1], op0=ALU.mult, op1=ALU.add)
                nc.vector.tensor_copy(key_all[:, :, span(PTOP * u, PTOP)], esel[:, :, :])
                dve.drain()
                nc.vector.tensor_copy(idx_all[:, span(PTOP * u, PTOP)], eidx[:, :]).then_inc(idx_ok, 1)
            elif step == 11:
                dve.wait_ge(ex_ok, u + 1)
                nc.vector.reciprocal(tsum[:, 1:2], tsum[:, 0:1])
            elif step == 12:
                nc.vector.tensor_scalar(cw_all[:, span(PTOP * u, PTOP)], texp[:, :], tsum[:, 1:2], 0.5, ALU.mult, ALU.mult)

        def dot(u, par, tile, k):
            dve.wait_ge(u_in[k % RING], 16 * (PTOP // RING) * u + 16 * (k // RING + 1))
            nc.vector.tensor_tensor_reduce(out=u_ring[:, k % RING], in0=u_ring[:, k % RING], in1=h2[:, tile], scale=1.0, scalar=0.0,
                                           op0=ALU.mult, op1=ALU.add, accum_out=dots[:, par, k:k + 1]).then_inc(dot_ok, 1)

        def gelu_argument(u, par):
            d = dots[:, par]
            dve.drain()
            nc.vector.tensor_tensor(gel[:, 0], d, d, ALU.mult)
            dve.drain()
            nc.vector.tensor_scalar(gel[:, 0], gel[:, 0], 0.044715, 1.0, ALU.mult, ALU.add)
            dve.drain()
            nc.vector.tensor_tensor(gel[:, 0], gel[:, 0], d, ALU.mult).then_inc(arg_ok, 1)

        def coefficients(u, par):
            dve.wait_ge(th_ok, u + 1)
            nc.vector.scalar_tensor_tensor(out=coef[:, par], in0=gel[:, 1], scalar=1.0, in1=dots[:, par], op0=ALU.add, op1=ALU.mult)
            dve.drain()
            w = cw_all[:, span(PTOP * u, PTOP)]
            nc.vector.tensor_tensor(w, coef[:, par], w, ALU.mult).then_inc(cw_ok, 1)

        def one_hot(G, par, tok, m):
            if m == 0:
                dve.wait_ge(c_pe, G - 1)
                nc.vector.tensor_tensor(ones[:, 1, par], iota_f[:, :].unsqueeze(1).to_broadcast([P, GTOK, P]),
                                        pickT[:, 1, span(tok, GTOK)].unsqueeze(2).to_broadcast([P, GTOK, P]), ALU.is_equal)
            last = nc.vector.tensor_scalar(ones[:, 0, par, m], iota_f[:, :], pickT[:, 0, span(tok, 1)], pickT[:, 2, span(tok, 1)],
                                           ALU.is_equal, ALU.mult)
            if m == GTOK - 1:
                last.then_inc(oh_ok, 1)

        def phase(c, par, tile, top=True):
            first = isinstance(c, int) and c == 0
            for k in range(PTOP):
                if k == 0 and not first:
                    gelu_argument(c - 1, 1 - par)
                dot(c, par, tile, k)
                if k == 0 and not first:
                    coefficients(c - 1, 1 - par)
                if k < PICK_STEPS and top:
                    pick_step(c + 1, k)

        for step in range(PICK_STEPS):
            pick_step(0, step)
        phase(0, 0, 0)
        phase(1, 1, 0)
        with dve.Fori(1, PH // 2) as i:
            for par in range(2):
                phase(2 * i + par, par, 0)
        with dve.Fori(PH // 2, PH - 1) as i:
            for par in range(2):
                phase(2 * i + par, par, 1)
        phase(NU - 2, 0, 1)
        phase(NU - 1, 1, 1, top=False)
        gelu_argument(NU - 1, 1)
        coefficients(NU - 1, 1)
        dve.wait_ge(pk_ev, 2)
        with dve.Fori(0, GROUPS // 2) as i:
            for par in range(2):
                for m in range(GTOK):
                    one_hot(2 * i + (GROUPS + par), par, 2 * GTOK * i + (GTOK * par + m), m)

        with dve.Fori(0, PKEYS // RING) as i:
            for j in range(RING):
                dve.wait_ge(vh_ok, RING * i + (j + 1))
                nc.vector.tensor_tensor(c_lo[:, j % NHL], ct[:, span(RING * i + j, 1)].rearrange("p a t -> p (a t)"),
                                        c_hi[:, j % NHL].bitcast(F32), ALU.subtract)
                nc.vector.tensor_tensor(v_lo[:, j % NHL], u_ring[:, j], v_hi[:, j % NHL].bitcast(F32), ALU.subtract).then_inc(vl_ok, 1)

        dve.wait_ge(res_in, 16)
        dve.wait_ge(fin_in, 16)
        for t in range(NT):
            dve.wait_ge(fin_pe, t + 1)
            nc.vector.tensor_tensor(x1f[:, t], x1f[:, t], ps[:, 4 * t:4 * t + 4, :].rearrange("p a b -> p (a b)"), ALU.add).then_inc(sum_ok, 1)
        for t in range(NT):
            mean_root(5 + t, 1, D)
            for h in range(2):
                cols = slice(D // 2 * h, D // 2 * (h + 1))
                nc.vector.scalar_tensor_tensor(out=outst[:, t, cols], in0=x1f[:, t, cols], scalar=stat[:, 5 + t, 6:7], in1=gfin[:, cols],
                                               op0=ALU.mult, op1=ALU.mult).then_inc(o_ok, 1)

    @block.tensor
    def _(pe):
        PRODUCTS = ((0, 0), (0, 1), (1, 0))
        w_parts, act_parts, mg_parts = (w_hi, w_lo), (act_hi, act_lo), (mg_hi, mg_lo)
        w_wide = [w[:, :, :, :].rearrange("p s (a b) c -> p s a (b c)", b=WIDE // P) for w in w_parts]

        def by_column(out_ap, slot, k0, k1, waits=None):
            for k in range(k0, k1):
                if waits is not None:
                    waits(k)
                for m, (wp, ap) in enumerate(PRODUCTS):
                    last = nc.tensor.matmul(out_ap, w_parts[wp][:, slot, k], act_parts[ap][:, k],
                                            start=(k == k0 and m == 0), stop=(k == k1 - 1 and m == 2))
            return last

        pe.wait_ge(ident_ok, 2)
        pe.wait_ge(const_in, 16 * 4)
        nc.tensor.transpose(ps[:, 6, 0:NK + 1], gain_rows[0:NK + 1, :], ident[0:NK + 1, 0:NK + 1]).then_inc(pre_pe, 1)
        pe.wait_ge(relx_ok, 1)
        nc.tensor.matmul(ps[0:16, 7, 0:384], relx[:, 0:16], onehot[:, 0], start=True, stop=True).then_inc(pre_pe, 1)
        nc.tensor.matmul(ps[0:16, 1, 0:384], relx[:, 16:32], onehot[:, 1], start=True, stop=True).then_inc(pre_pe, 1)
        pe.wait_ge(xn_ok, NT)
        for k in range(NK):
            wait(pe, xt_lo, k - 3)
            for t in range(NT):
                last = nc.tensor.transpose(ps[:, 2 + k % 4, P * t:P * t + P], xin[:, t, P * k:P * k + P], ident[:, :])
            last.then_inc(xt_pe, 1)
        pe.wait_ge(xt_lo, NK)
        pe.wait_ge(pre_ev, 3)

        def logits(unit):
            pe.wait_ge(evac_done, 4)
            wait(pe, lg_ev, unit - 1)
            t, heads, width = (0, range(4 * unit, 4 * unit + 4), P) if unit < 2 else (1, range(2 * unit - 4, 2 * unit - 2), T)
            for m, h in enumerate(heads):
                last = nc.tensor.matmul(ps[:, S_BANK + unit % 2, width * m:width * m + width], iqT[:, h // 4, P * t:P * t + P],
                                        ikz[:, h % 4, 0:width], start=True, stop=True)
            last.then_inc(lg_pe, 1)

        def turn(n):
            r = TURNED.index(n)
            pe.wait_ge(evac_done, n + 1)
            wait(pe, turn_ev, r - 1)
            if r == 1:
                pe.wait_ge(up_ev, 4)
            for t in range(NT):
                last = nc.tensor.transpose(ps[:, PT_BANK + r % 2, P * t:P * t + P], turn_st[:, r % 2, P * t:P * t + P], ident[:, :])
            last.then_inc(turn_pe, 1)

        for n in range(N_FIRST):
            pe.wait_ge(lo_done, n + 1)
            wait(pe, evac_done, n - 1)
            bank, slot = ps[:, J + n % 2], n % NHL
            by_column(bank[:, 0:T], slot, 0, NK).then_inc(blk_done, 1)
            if n - 1 in TURNED:
                turn(n - 1)
            if n == 3:
                pe.wait_ge(cn_ok, NT)
                for t in range(NT):
                    last = nc.tensor.transpose(ps[:, T_BANK, P * t:P * t + P], clat[:, t], ident[:, :])
                last.then_inc(ct_pe, 1)
                for t in range(NT):
                    last = nc.tensor.transpose(ps[:, O_BANK, P * t:P * t + P], ikwT[:, P * t:P * t + P], ident[:, :])
                last.then_inc(ct_pe, 1)
            if n == 4:
                pe.wait_ge(uk_in, 32)
                pe.wait_ge(ct_ev, 2)
                for j in range(2):
                    for m in range(2):
                        c = P * (2 * j + m)
                        last = nc.tensor.matmul(ps[:, 6 + j, T * m:T * m + T], w_uk[:, c:c + P], cT[:, :], start=True, stop=True)
                    last.then_inc(up_pe, 1)
                for t in range(NT):
                    nc.tensor.matmul(ps[:, 4 + t, :], cT[:, P * t:P * t + P], w_uv[:, :], start=True, stop=True).then_inc(up_pe, 1)
            if 5 <= n < 11:
                if n == 5:
                    pe.wait_ge(pads_ok, 2)
                logits(n - 5)
        turn(N_FIRST - 1)
        pe.wait_ge(lg_ev, 6)
        pe.wait_ge(turn_ev, len(TURNED))

        def body(kind, i, b):
            n0 = 8 * b + N_FIRST

            def weights(j):
                pe.wait_ge(lo_done, n0 + (j + 1))
                pe.wait_ge(evac_done, n0 + (j - 1))
                by_column(ps[:, J + j % 2, 0:T], j % NHL, 0, NK).then_inc(blk_done, 1)

            def scores(par):
                pe.wait_ge(q_ready, 2 * b + (par + 1))
                pe.wait_ge(evac_done, n0 + (par + 1))
                wait(pe, s_read, 2 * b + par)
                key = T * i if kind == "a" else 2 * T * i + T * ((KT_B if kind == "b" else KT_C) + par)
                for hh in range(2):
                    nc.tensor.matmul(ps[:, S_BANK + hh, 0:T], q_st[:, par, hh, P:T], kT[:, span(key, T)], start=True, stop=True)
                    last = nc.tensor.matmul(ps[:, S_BANK + hh, T:3 * P], q_st[:, par, hh, 0:P], kT[:, span(key, P)], start=True, stop=True)
                last.then_inc(s_done, 1)

            def turn_probs(par):
                pe.wait_ge(e_done, 2 * b + (par + 1))
                wait(pe, pt_ev, 2 * b + par)
                for hh in range(2):
                    for c in range(3):
                        last = nc.tensor.transpose(ps[:, PT_BANK + hh, P * c:P * c + P], probs[:, par, hh, P * c:P * c + P], ident[:, :])
                last.then_inc(pt_done, 1)

            def values(par):
                pe.wait_ge(pt_ev, 2 * b + (par + 1))
                wait(pe, o_done, 2 * b + par)
                for hh in range(2):
                    col = HD * i if kind == "a" else 2 * P * i + ((V_B if kind == "b" else V_C) + P * par + HD * hh)
                    nc.tensor.matmul(ps[:, O_BANK, HD * hh:HD * hh + HD], pT[:, hh, T:3 * P], vals[:, 0, span(col, HD)], start=True, stop=True)
                    for s in range(NT):
                        last = nc.tensor.matmul(ps[:, O_BANK, P + HD * hh:P + HD * hh + HD], pT[:, hh, P * s:P * s + P],
                                                vals[:, s, span(col, HD)], start=(s == 0), stop=(s == NT - 1))
                last.then_inc(pv_done, 1)

            def turn_outs(par):
                pe.wait_ge(o_done, 2 * b + (par + 1))
                wait(pe, y_ev, 2 * b + par)
                for t in range(NT):
                    last = nc.tensor.transpose(ps[:, T_BANK, P * t:P * t + P], o_st[:, t], ident[:, :])
                last.then_inc(ot_done, 1)

            weights(0)
            weights(1)
            scores(0)
            weights(2)
            scores(1)
            weights(3)
            turn_probs(0)
            weights(4)
            turn_probs(1)
            values(0)
            weights(5)
            values(1)
            turn_outs(0)
            weights(6)
            turn_outs(1)
            weights(7)
        attention_bodies(pe, body)

        pe.wait_ge(evac_done, N_BR)

        def merge(i):
            for j in range(NRAW):
                pe.wait_ge(lo_done, NRAW * i + (N_BR + j + 1))
                wait(pe, m_mul, NRAW * i + (j - 1))
                waits = None
                if isinstance(i, int) and j == 0:
                    waits = lambda k: pe.wait_ge(y_lo, k // 4 + 1)
                by_column(ps[:, J + j % 2, 0:T], j % NHL, 0, 8, waits)
                by_column(ps[:, J + j % 2, T:2 * T], j % NHL, 8, 12, waits)
                by_column(ps[:, S_BANK + j % 2, 0:T], j % NHL, 12, NK, waits).then_inc(blk_done, 1)
        peeled(pe, NK // NRAW, merge)
        pe.wait_ge(m_mul, NK)

        for c in range(NWIDE):
            wait(pe, x1_ok, c - 1)
            for j in range(NRAW):
                pe.wait_ge(lo_done, NRAW * c + N_OUT + j + 1)
                if c == 0:
                    pe.wait_ge(m_lo, NRAW * (j + 1))
                for t in range(NT):
                    for kk in range(NRAW):
                        k = NRAW * j + kk
                        for m, (wp, ap) in enumerate(PRODUCTS):
                            last = nc.tensor.matmul(ps[:, 2 * (c % 2) + t, :], mg_parts[ap][:, T * k + P * t:T * k + P * t + P],
                                                    w_wide[wp][:, j % NHL, kk], start=(k == 0 and m == 0), stop=(k == NK - 1 and m == 2))
                last.then_inc(blk_done, 1)
            if c == NWIDE - 2:
                pe.wait_ge(sk_in, 16)
                for n in range(4):
                    for m in range(4):
                        last = nc.tensor.transpose(ps[:, SK_BANK + n, P * m:P * m + P], subk[:, 4 * n + m], ident[:, :])
                    last.then_inc(sk_pe, 1)
        pe.wait_ge(sk_ev, 4)

        def turn_h2(t):
            pe.wait_ge(h2_ok, t + 1)
            for kg in range(4):
                wait(pe, ht_ev, 4 * t + kg - 3)
                for m in range(4):
                    k = 4 * kg + m
                    last = nc.tensor.transpose(ps[:, SK_BANK + kg, P * m:P * m + P], h2[:, t, P * k:P * k + P], ident[:, :])
                last.then_inc(ht_pe, 1)

        def query_block(w, cols):
            for k in range(NK):
                last = nc.tensor.matmul(ps[:, J + w % 2, cols], wq_raw[:, (w + NWQ // 2) % NWQ, k], h2T[:, k, cols], start=(k == 0), stop=(k == NK - 1))
            return last

        def key_scores(w, t):
            return nc.tensor.matmul(ps[:, S_BANK + w % 2, P * t:P * t + P], qp_st[:, w % 2, P * t:P * t + P],
                                    subkT[:, w], start=True, stop=True)

        turn_h2(0)
        pe.wait_ge(ht_ev, 4)
        for j in range(2):
            pe.wait_ge(wq_in[j], 16)
            query_block(j, slice(0, P)).then_inc(hq_pe, 1)
        for j in range(2):
            pe.wait_ge(hq_ev, j + 1)
            key_scores(j, 0).then_inc(hq_pe, 1)
        turn_h2(1)
        pe.wait_ge(ht_ev, 8)
        for j in range(2):
            query_block(j, slice(P, T)).then_inc(blk_done, 1)
        for j in range(2):
            pe.wait_ge(qp_ev, j + 1)
            pe.wait_ge(hq_ev, 3 + j)
            key_scores(j, 1).then_inc(s2_pe, 1)

        for w in range(2, 2 * PH):
            pe.wait_ge(wq_in[w % NWQ], 16 * (w // NWQ + 1))
            pe.wait_ge(qp_ev, w - 1)
            query_block(w, slice(0, T)).then_inc(blk_done, 1)
            pe.wait_ge(qp_ev, w + 1)
            pe.wait_ge(s2_ev, w - 1)
            for t in range(NT):
                last = key_scores(w, t)
            last.then_inc(s2_pe, 1)
        pe.wait_ge(s2_ev, 2 * PH)

        def turn_picks(tile):
            pe.wait_ge(cw_ok, PH * (tile + 1))
            cols = slice(PICKS * tile, PICKS * (tile + 1))
            for m, src in enumerate((key_all[:, 0, cols], key_all[:, 1, cols], cw_all[:, cols])):
                last = nc.tensor.transpose(ps[:, 5, P * m:P * m + P], src, ident[:, :])
            last.then_inc(pk_pe, 1)

        def matrices(G, par):
            pe.wait_ge(oh_ok, G + 1)
            wait(pe, c_ev, G - 1)
            for m in range(GTOK):
                last = nc.tensor.matmul(ps[:, 6 + par, PKEYS * m:PKEYS * m + PKEYS], ones[:, 1, par, m], ones[:, 0, par, m], start=True, stop=True)
            last.then_inc(c_pe, 1)

        turn_picks(0)
        for par in range(2):
            matrices(par, par)
        with pe.Fori(1, GROUPS // 2) as i:
            for par in range(2):
                matrices(2 * i + par, par)
        turn_picks(1)
        with pe.Fori(GROUPS // 2, GROUPS) as i:
            for par in range(2):
                matrices(2 * i + par, par)
        pe.wait_ge(c_ev, NT * GROUPS)

        v_parts, c_parts = (v_hi, v_lo), (c_hi, c_lo)

        def add_block(i, first=False, final=False):
            for j in range(RING):
                pe.wait_ge(vl_ok, RING * i + (j + 1))
                for t in range(NT):
                    for c in range(4):
                        for m, (vp, cp) in enumerate(PRODUCTS):
                            last = nc.tensor.matmul(ps[:, 4 * t + c, :], c_parts[cp][:, j % NHL, P * t:P * t + P],
                                                    v_parts[vp][:, j % NHL, WIDE * c:WIDE * c + WIDE],
                                                    start=(first and j == 0 and m == 0), stop=(final and j == RING - 1 and m == 2))
                    if final and j == RING - 1:
                        last.then_inc(fin_pe, 1)
                if not (final and j == RING - 1):
                    last.then_inc(acc_ok, 1)

        add_block(0, first=True)
        with pe.Fori(1, PKEYS // RING - 1) as i:
            add_block(i)
        add_block(PKEYS // RING - 1, final=True)


_INS = ["x", "rel_bias", "g_mix", "w_in", "a_sinks", "c_lat_gain", "c_w_uk", "c_w_uv", "w_br_a", "w_br_b", "w_br_c",
        "w_out", "g_ffn", "peer_w_q", "peer_sub_keys", "peer_u", "peer_v", "g_final"]


def kernel(**inputs):
    import numpy as _np
    import concourse.bacc as _bacc
    from concourse import mybir as _mybir
    from concourse.bass_utils import run_bass_kernel_spmd as _run

    nc = _bacc.Bacc("TRN2", target_bir_lowering=False, num_devices=1)
    arrays, args = {}, []
    for name in _INS:
        a = _np.ascontiguousarray(inputs[name])
        arrays[f"in_{name}"] = a
        args.append(nc.dram_tensor(f"in_{name}", a.shape, _mybir.dt.from_np(a.dtype), kind="ExternalInput").ap())
    args.append(nc.dram_tensor("out_0", (1, T, D), F32, kind="ExternalOutput").ap())
    build(nc, *args)
    r = _run(nc, [arrays], core_ids=[0])
    return r.results[0]["out_0"]
```
